# Optimizing a Trainium2 kernel written in Bass

```python
import jax, jax.numpy as jnp
from jax import lax
import numpy as np

D_MODEL = 1024
BATCH = 1
SEQ = 1024
DEPTH = 1
DEC_BATCH = 8
DEC_SEQ = 1
PAST_LEN = 8192
PAGE_SIZE = 128

CONV_DIM = D_MODEL // 2
CONV_W = 3
SGU_DIM = D_MODEL - CONV_DIM
SGU_GROUPS = 4
SGU_GROUP_DIM = SGU_DIM // SGU_GROUPS
CHUNK = 128
IN_DIM = 3 * CONV_DIM + 2 * SGU_DIM
PEER_HEADS = 8
N_KEYS = 128
N_EXPERTS = N_KEYS * N_KEYS
PEER_TOPK = 16
D_QUERY = 256
D_HALF = D_QUERY // 2
TOKEN_BLOCK = 128
EPS = 1e-6

kernel_name = 'hybrid_conv_sgu_peer_decode_step'

def rms_norm(x, g):
    x32 = x.astype(jnp.float32)
    y = x32 * lax.rsqrt(jnp.mean(x32 * x32, axis=-1, keepdims=True) + EPS)
    return (y * g.astype(jnp.float32)).astype(x.dtype)

def group_layer_norm(v, g):
    v32 = v.astype(jnp.float32)
    mu = jnp.mean(v32, axis=-1, keepdims=True)
    d = v32 - mu
    y = d * lax.rsqrt(jnp.mean(d * d, axis=-1, keepdims=True) + EPS)
    return (y * g.astype(jnp.float32).reshape(SGU_GROUPS, SGU_GROUP_DIM)).astype(v.dtype)

def ada_params(c, w_ada, b_ada):
    m = jnp.einsum('bd,de->be', jax.nn.silu(c), w_ada) + b_ada
    return jnp.split(m[:, None, :], 6, axis=-1)

def short_conv_mixer(b_gate, c_gate, h, prefix, conv_w):
    z = c_gate * h
    zp = jnp.concatenate([prefix.astype(z.dtype), z], axis=1)
    L = z.shape[1]
    y = zp[:, 0:L] * conv_w[:, 0]
    for k in range(1, CONV_W):
        y = y + zp[:, k:k + L] * conv_w[:, k]
    return b_gate * y, zp[:, -(CONV_W - 1):]

def chunk_sgu(u, v, sgu_norm_g, w_s, b_s):
    bn, L, _ = v.shape
    vn = group_layer_norm(v.reshape(bn, L, SGU_GROUPS, SGU_GROUP_DIM), sgu_norm_g)
    n_chunks = -(-L // CHUNK)
    pad = n_chunks * CHUNK - L
    vp = jnp.pad(vn, ((0, 0), (0, pad), (0, 0), (0, 0))).reshape(
        bn, n_chunks, CHUNK, SGU_GROUPS, SGU_GROUP_DIM)
    w_causal = jnp.tril(w_s)
    mixed = jnp.einsum('gts,bnsgc->bntgc', w_causal, vp) + b_s.T[None, None, :, :, None]
    mixed = mixed.reshape(bn, n_chunks * CHUNK, SGU_DIM)[:, :L]
    return u * mixed, vn.reshape(bn, L, SGU_DIM)

def peer_block(xb, w_q, sub_keys, expert_u, expert_v):
    tb = xb.shape[0]
    q = jnp.einsum('td,de->te', xb, w_q).reshape(tb, PEER_HEADS, 2, D_HALF)
    s = jnp.einsum('thpc,hpkc->thpk', q, sub_keys).astype(jnp.float32)
    sv, si = lax.top_k(s, PEER_TOPK)
    cand = sv[:, :, 0, :, None] + sv[:, :, 1, None, :]
    cv, ci = lax.top_k(cand.reshape(tb, PEER_HEADS, PEER_TOPK * PEER_TOPK), PEER_TOPK)
    i1 = jnp.take_along_axis(si[:, :, 0, :], ci // PEER_TOPK, axis=-1)
    i2 = jnp.take_along_axis(si[:, :, 1, :], ci % PEER_TOPK, axis=-1)
    expert = (i1 * N_KEYS + i2).reshape(tb, PEER_HEADS * PEER_TOPK)
    g = jax.nn.softmax(cv, axis=-1).reshape(tb, PEER_HEADS * PEER_TOPK)
    act = jax.nn.gelu(jnp.einsum('tkd,td->tk', expert_u[expert], xb).astype(jnp.float32),
                      approximate=False)
    w = (g * act).astype(xb.dtype)
    return jnp.einsum('tk,tkd->td', w, expert_v[expert])

def peer_ffn(x, w_q, sub_keys, expert_u, expert_v):
    bn, L, d = x.shape
    t = bn * L
    nb = -(-t // TOKEN_BLOCK)
    xt = jnp.pad(x.reshape(t, d), ((0, nb * TOKEN_BLOCK - t), (0, 0))).reshape(nb, TOKEN_BLOCK, d)
    y = lax.map(lambda xb: peer_block(xb, w_q, sub_keys, expert_u, expert_v), xt)
    return y.reshape(nb * TOKEN_BLOCK, d)[:t].reshape(bn, L, d)

def layer(x, c, conv_prefix, w_ada, b_ada, g_pre_mix, w_in, conv_w, sgu_norm_g, w_s, b_s,
          w_out, g_post_mix, g_pre_ffn, w_q, sub_keys, expert_u, expert_v, g_post_ffn):
    sh1, sc1, gt1, sh2, sc2, gt2 = ada_params(c, w_ada, b_ada)
    h = rms_norm(x, g_pre_mix) * (1 + sc1) + sh1
    p = jnp.einsum('bld,de->ble', h, w_in)
    b_gate, c_gate, hc, u, v = jnp.split(
        p, [CONV_DIM, 2 * CONV_DIM, 3 * CONV_DIM, 3 * CONV_DIM + SGU_DIM], axis=-1)
    yc, conv_state = short_conv_mixer(b_gate, c_gate, hc, conv_prefix, conv_w)
    ys, v_rows = chunk_sgu(u, v, sgu_norm_g, w_s, b_s)
    mix = jnp.einsum('ble,ed->bld', jnp.concatenate([yc, ys], axis=-1), w_out)
    x = x + gt1 * rms_norm(mix, g_post_mix)
    h2 = rms_norm(x, g_pre_ffn) * (1 + sc2) + sh2
    x = x + gt2 * rms_norm(peer_ffn(h2, w_q, sub_keys, expert_u, expert_v), g_post_ffn)
    return x, conv_state, v_rows

def setup_inputs(seed: int = 0) -> dict:
    key = jax.random.key(seed)
    ks = jax.random.split(key, 24)

    def nrm(k, shape, scale):
        return jax.random.normal(k, shape, jnp.float32) * scale

    return {
        'x_prompt': nrm(ks[0], (BATCH, SEQ, D_MODEL), 1.0),
        'x_sample': nrm(ks[1], (DEC_BATCH, DEC_SEQ, D_MODEL), 1.0),
        'state_conv': nrm(ks[2], (DEPTH, DEC_BATCH, CONV_W - 1, CONV_DIM), 1.0),
        'c_prompt': nrm(ks[3], (BATCH, D_MODEL), 1.0),
        'c_sample': nrm(ks[4], (DEC_BATCH, D_MODEL), 1.0),
        'w_ada': nrm(ks[5], (DEPTH, D_MODEL, 6 * D_MODEL), 0.5 * D_MODEL ** -0.5),
        'b_ada': nrm(ks[6], (DEPTH, 6 * D_MODEL), 0.01),
        'g_pre_mix': 1.0 + nrm(ks[7], (DEPTH, D_MODEL), 0.05),
        'w_in': nrm(ks[8], (DEPTH, D_MODEL, IN_DIM), D_MODEL ** -0.5),
        'conv_w': nrm(ks[9], (DEPTH, CONV_DIM, CONV_W), CONV_W ** -0.5),
        'sgu_norm_g': 1.0 + nrm(ks[10], (DEPTH, SGU_DIM), 0.05),
        'w_s': nrm(ks[11], (DEPTH, SGU_GROUPS, CHUNK, CHUNK), CHUNK ** -0.5),
        'b_s': 1.0 + nrm(ks[12], (DEPTH, SGU_GROUPS, CHUNK), 0.1),
        'w_out': nrm(ks[13], (DEPTH, D_MODEL, D_MODEL), D_MODEL ** -0.5),
        'g_post_mix': 1.0 + nrm(ks[14], (DEPTH, D_MODEL), 0.05),
        'g_pre_ffn': 1.0 + nrm(ks[15], (DEPTH, D_MODEL), 0.05),
        'w_q': nrm(ks[16], (DEPTH, D_MODEL, PEER_HEADS * D_QUERY), D_MODEL ** -0.5),
        'sub_keys': nrm(ks[17], (DEPTH, PEER_HEADS, 2, N_KEYS, D_HALF), D_HALF ** -0.5),
        'expert_u': nrm(ks[18], (DEPTH, N_EXPERTS, D_MODEL), D_MODEL ** -0.5),
        'expert_v': nrm(ks[19], (DEPTH, N_EXPERTS, D_MODEL), D_MODEL ** -0.5),
        'g_post_ffn': 1.0 + nrm(ks[20], (DEPTH, D_MODEL), 0.05),
    }

def reference(x_prompt, x_sample, state_conv, c_prompt, c_sample, w_ada, b_ada, g_pre_mix,
              w_in, conv_w, sgu_norm_g, w_s, b_s, w_out, g_post_mix, g_pre_ffn, w_q,
              sub_keys, expert_u, expert_v, g_post_ffn):
    xp, xs = x_prompt, x_sample
    conv_p, conv_s, v_s = [], [], []
    for l in range(DEPTH):
        params = (w_ada[l], b_ada[l], g_pre_mix[l], w_in[l], conv_w[l], sgu_norm_g[l], w_s[l],
                  b_s[l], w_out[l], g_post_mix[l], g_pre_ffn[l], w_q[l], sub_keys[l],
                  expert_u[l], expert_v[l], g_post_ffn[l])
        zero_prefix = jnp.zeros((xp.shape[0], CONV_W - 1, CONV_DIM), xp.dtype)
        xp, cst_p, _ = layer(xp, c_prompt, zero_prefix, *params)
        xs, cst_s, v_rows_s = layer(xs, c_sample, state_conv[l], *params)
        conv_p.append(cst_p)
        conv_s.append(cst_s)
        v_s.append(v_rows_s)
    new_conv_prompt = jnp.stack(conv_p)
    new_conv_sample = jnp.stack(conv_s)
    sgu_v_sample = jnp.stack(v_s)
    return (xp, xs, new_conv_prompt, new_conv_sample, sgu_v_sample)


_drawn_inputs = setup_inputs


def setup_inputs(seed=0):
    import zlib

    import numpy as np

    out = dict(_drawn_inputs(seed))
    spreads = {}
    factors = {'g_post_ffn': 4.083}
    for name, (base, spread) in spreads.items():
        noise = np.random.default_rng([zlib.crc32(name.encode()), seed]).standard_normal(out[name].shape)
        drawn = base * np.exp(spread * noise) if base else spread * noise
        out[name] = __import__('jax').numpy.asarray(drawn.astype(out[name].dtype))
    for name, factor in factors.items():
        out[name] = (out[name] * factor).astype(out[name].dtype)
    return out
```

```python
import numpy as np
from contextlib import ExitStack

import concourse.bass as bass
from concourse import mybir

F32 = mybir.dt.float32
BF16 = mybir.dt.bfloat16
U32 = mybir.dt.uint32
ALU = mybir.AluOpType
ACT = mybir.ActivationFunctionType
AX = mybir.AxisListType.X
ds = bass.ds

P = 128
D = 1024
KD = D // P
SEQ = 1024
NS = 8
CONV = 512
CB = CONV // P
G = 4
IN_DIM = 3 * CONV + 2 * CONV
HEADS = 8
KEYS = 128
TOPK = 16
HALF = 512
TB = HALF // P
NBLK = SEQ // P + 1
EPS = 1e-6
LOWEST = -3.0e38

SHIFT1, SCALE1, GATE1, SHIFT2, SCALE2, GATE2 = range(6)


def wait_apart(eng, noted, *waits):
    for sem, value in waits:
        eng.wait_ge(sem, value)
    eng.sem_inc(noted, 1)


class Steps:

    def __init__(self, eng, sem, base=0, noted=None):
        self.eng, self.sem, self.base, self.n, self.noted = eng, sem, base, 0, noted

    def did(self, ins):
        ins.then_inc(self.sem, 1)
        self.n += 1
        return ins

    def settle(self):
        if self.noted is not None:
            wait_apart(self.eng, self.noted, (self.sem, self.base + self.n))
        else:
            self.eng.wait_ge(self.sem, self.base + self.n)


def build(nc, t):
    scratch = {
        "mod": nc.dram_tensor("mod_rows", (9, 6, D), F32, kind="Internal").ap(),
        "x1": nc.dram_tensor("x1_rows", (NBLK * P, D), F32, kind="Internal").ap(),
        "h2": nc.dram_tensor("h2_rows", (NBLK * P, D), F32, kind="Internal").ap(),
        "h2_parts": nc.dram_tensor("h2_part_rows", (3, NBLK * P, D), BF16, kind="Internal").ap(),
    }
    with ExitStack() as ctx:
        ident = ctx.enter_context(nc.sbuf_tensor("ident", [P, P], F32))
        with ExitStack() as weights:
            w_in = weights.enter_context(nc.sbuf_tensor("w_in", [P, KD, IN_DIM], F32))
            wsT = weights.enter_context(nc.sbuf_tensor("wsT", [P, G, P], F32))
            condition(nc, t, scratch, ident, w_in, wsT)
            mix_prompt(nc, t, scratch, ident, w_in, wsT)
            mix_sample(nc, t, scratch, ident, w_in)
        peer(nc, t, scratch, ident)


def condition(nc, t, scratch, ident, w_in, wsT):
    ROWS = NS + 1
    CHUNKS = 6 * D // HALF
    RING = 3
    with ExitStack() as ctx:
        def sb(name, shape, dt=F32):
            return ctx.enter_context(nc.sbuf_tensor(name, shape, dt))

        def sem(name):
            return ctx.enter_context(nc.semaphore(name))

        c_rows = sb("c_rows", [ROWS, D])
        c_act = sb("c_act", [ROWS, D])
        cT = sb("cT", [P, KD, ROWS])
        ada_w = [sb(f"ada_w{r}", [P, KD, HALF]) for r in range(RING)]
        ada_b = sb("ada_b", [ROWS, 6 * D])
        mod = sb("mod", [ROWS, 6, D])
        mod_flat = mod[:, :, :].rearrange("p a b -> p (a b)")
        gains = sb("gains", [ROWS, 3, D])
        w_s = sb("w_s", [P, G, P])
        ps_cT = ctx.enter_context(nc.psum_tensor("ps_cT", [P, KD, ROWS], F32))
        ps_wsT = ctx.enter_context(nc.psum_tensor("ps_wsT", [P, G, P], F32))
        ps_ada = [ctx.enter_context(nc.psum_tensor(f"ps_ada{r}", [ROWS, HALF], F32)) for r in range(RING)]

        c_landed = sem("c_landed")
        b_landed = sem("b_landed")
        gains_landed = sem("gains_landed")
        ws_landed = sem("ws_landed")
        win_landed = sem("win_landed")
        ada_landed = [sem(f"ada_landed{r}") for r in range(RING)]
        silu_done = sem("silu_done")
        const_done = sem("const_done")
        cT_done = sem("cT_done")
        cT_copied = sem("cT_copied")
        ws_masked = sem("ws_masked")
        ws_turned = sem("ws_turned")
        ws_copied = sem("ws_copied")
        ada_done = [sem(f"ada_done{r}") for r in range(RING)]
        ada_added = [sem(f"ada_added{r}") for r in range(RING)]
        mod_step = sem("mod_step")
        mod_stored = sem("mod_stored")
        block = ctx.enter_context(nc.Block())

        @block.sync
        def _(sp):
            sp.dma_start(c_rows[0:NS, :], t["c_sample"]).then_inc(c_landed, 16)
            sp.dma_start(c_rows[NS:ROWS, :], t["c_prompt"]).then_inc(c_landed, 16)
            with sp.Fori(0, CHUNKS // RING) as n:
                for r in range(RING):
                    sp.wait_ge(ada_done[r], 1 + n)
                    sp.dma_start(ada_w[r][:, :, :],
                                 t["w_ada"][0].rearrange("(k p) n -> p k n", p=P)[:, :, ds((n * RING + r) * HALF, HALF)]
                                 ).then_inc(ada_landed[r], 16)
            sp.dma_start(w_in[:, :, :], t["w_in"][0].rearrange("(k p) n -> p k n", p=P)).then_inc(win_landed, 16)
            sp.wait_ge(mod_step, 3)
            sp.dma_start(scratch["mod"], mod[:, :, :]).then_inc(mod_stored, 16)
            sp.wait_ge(mod_stored, 16)
            sp.wait_ge(win_landed, 16)

        @block.scalar
        def _(act):
            act.dma_start(ada_b[:, :], t["b_ada"][0:1, :].to_broadcast([ROWS, 6 * D])).then_inc(b_landed, 16)
            for n, name in enumerate(("g_pre_mix", "g_post_mix", "g_pre_ffn")):
                act.dma_start(gains[:, n, :], t[name][0:1, :].to_broadcast([ROWS, D])).then_inc(gains_landed, 16)
            act.dma_start(w_s[:, :, :], t["w_s"][0].rearrange("g t s -> t g s")).then_inc(ws_landed, 16)
            act.wait_ge(c_landed, 32)
            nc.scalar.activation(c_act[:, :], c_rows[:, :], ACT.Silu).then_inc(silu_done, 1)

        @block.gpsimd
        def _(pool):
            pool.memset(ident[:, :], 0.0).then_inc(const_done, 1)
            pool.wait_ge(const_done, 1)
            pool.affine_select(out=ident[:, :], in_=ident[:, :], compare_op=ALU.not_equal, fill=1.0, base=0,
                               pattern=[[-1, P]], channel_multiplier=1).then_inc(const_done, 1)
            pool.wait_ge(ws_landed, 16)
            pool.affine_select(out=w_s[:, :, :], in_=w_s[:, :, :], compare_op=ALU.is_ge, fill=0.0, base=0,
                               pattern=[[0, G], [-1, P]], channel_multiplier=1).then_inc(ws_masked, 1)

        @block.tensor
        def _(pe):
            for primed in ada_done:
                pe.sem_inc(primed, 1)
            pe.wait_ge(const_done, 2)
            pe.wait_ge(silu_done, 1)
            for k in range(KD):
                last = pe.transpose(ps_cT[:, k, :], c_act[:, k * P:(k + 1) * P], ident[0:ROWS, 0:ROWS])
            last.then_inc(cT_done, 1)
            pe.wait_ge(ws_masked, 1)
            for g in range(G):
                last = pe.transpose(ps_wsT[:, g, :], w_s[:, g, :], ident[:, :])
            last.then_inc(ws_turned, 1)
            pe.wait_ge(cT_copied, 1)
            with pe.Fori(0, CHUNKS // RING) as n:
                for r in range(RING):
                    pe.wait_ge(ada_landed[r], 16 * n + 16)
                    pe.wait_ge(ada_added[r], 1 + n)
                    for k in range(KD):
                        last = pe.matmul(ps_ada[r][:, :], cT[:, k, :], ada_w[r][:, k, :],
                                         start=(k == 0), stop=(k == KD - 1))
                    last.then_inc(ada_done[r], 1)

        @block.vector
        def _(dve):
            for primed in ada_added:
                dve.sem_inc(primed, 1)
            dve.wait_ge(cT_done, 1)
            dve.tensor_copy(cT[:, :, :], ps_cT[:, :, :]).then_inc(cT_copied, 1)
            dve.wait_ge(ws_turned, 1)
            dve.tensor_copy(wsT[:, :, :], ps_wsT[:, :, :]).then_inc(ws_copied, 1)
            dve.wait_ge(b_landed, 16)
            with dve.Fori(0, CHUNKS // RING) as n:
                for r in range(RING):
                    dve.wait_ge(ada_done[r], 1 + n + 1)
                    cols = ds((n * RING + r) * HALF, HALF)
                    dve.tensor_tensor(mod_flat[:, cols], ps_ada[r][:, :], ada_b[:, cols], ALU.add
                                      ).then_inc(ada_added[r], 1)
            dve.wait_ge(gains_landed, 48)
            for r in range(RING):
                dve.wait_ge(ada_added[r], 1 + CHUNKS // RING)
            for dst, g in ((SCALE1, 0), (SCALE2, 2)):
                dve.scalar_tensor_tensor(out=mod[:, dst, :], in0=mod[:, dst, :], scalar=1.0, in1=gains[:, g, :],
                                         op0=ALU.add, op1=ALU.mult).then_inc(mod_step, 1)
            dve.tensor_tensor(mod[:, GATE1, :], mod[:, GATE1, :], gains[:, 1, :], ALU.mult).then_inc(mod_step, 1)


def mix_prompt(nc, t, scratch, ident, w_in, wsT):
    with ExitStack() as ctx:
        def sb(name, shape, dt=F32):
            return ctx.enter_context(nc.sbuf_tensor(name, shape, dt))

        def sem(name):
            return ctx.enter_context(nc.semaphore(name))

        w_out = sb("w_out", [P, KD, D])
        hT = sb("hT", [P, KD, HALF])
        yT = sb("yT", [P, KD, HALF])
        z = sb("z", [P, CB, 2 + HALF])
        x_in = [sb(f"x_in{i}", [P, D]) for i in range(2)]
        rows = [sb(f"rows{i}", [P, D]) for i in range(2)]
        x1w, h2w = rows
        gate1_b = sb("gate1_b", [P, D])
        scale2_b = sb("scale2_b", [P, D])
        shift2_b = sb("shift2_b", [P, D])
        scale1_f = sb("scale1_f", [P, KD])
        shift1_f = sb("shift1_f", [P, KD])
        conv_w = sb("conv_w_f", [P, CB, 3])
        v_dev = sb("v_dev", [P, CONV])
        v_sq = sb("v_sq", [P, CONV])
        v_norm = sb("v_norm", [P, CONV])
        v_gain = sb("v_gain", [P, CONV])
        c_sb, y_sb = v_dev, v_sq
        bs_row = sb("bs_row", [1, CONV])
        ones_row = sb("ones_row", [1, P])
        eps = sb("eps", [P, 1])
        junk = sb("junk", [P, D], BF16)
        parts = sb("parts", [P, 3, D], BF16)
        rest = sb("rest", [P, D])
        stat = sb("stat", [P, 3, 3])
        gstat = sb("gstat", [P, 5, G])
        banks = [ctx.enter_context(nc.psum_tensor(f"mix_bank{i}", [P, HALF], F32)) for i in range(2)]
        pair = [ctx.enter_context(nc.psum_tensor(f"mix_pair{i}", [P, D], F32)) for i in range(3)]
        ps_v, ps_mixed = banks
        ps_c, ps_h = pair[2][:, 0:HALF], pair[2][:, HALF:D]
        ps_b = pair[0][:, 0:HALF]
        ps_u = [pair[1][:, 0:HALF], pair[1][:, HALF:D]]
        ps_o = [pair[0], pair[2]]

        weights_landed = sem("weights_landed")
        mods_landed = sem("mods_landed")
        x_landed = [sem(f"x_landed{i}") for i in range(2)]
        xr_landed = [sem(f"xr_landed{i}") for i in range(2)]
        const_done = sem("mconst_done")
        ssq_done = sem("ssq_done")
        dve_x = sem("dve_x")
        xn_done = sem("xn_done")
        xT_done = sem("xT_done")
        hT_done = sem("hT_done")
        v_done = sem("v_done")
        dve_v = sem("dve_v")
        var_ready = sem("var_ready")
        vstd_done = sem("vstd_done")
        vn_done = sem("vn_done")
        mixed_done = sem("mixed_done")
        mixed_kept = sem("mixed_kept")
        c_done = sem("c_done")
        h_done = sem("h_done")
        b_done = sem("b_done")
        c_copied = sem("c_copied")
        dve_conv = sem("dve_conv")
        conv_done = sem("conv_done")
        u_done = sem("u_done")
        gated_done = sem("gated_done")
        tail_moved = sem("tail_moved")
        o_done = sem("o_done")
        ossq_done = sem("ossq_done")
        dve_o = sem("dve_o")
        o_used = sem("o_used")
        x1_done = sem("x1_done")
        x1ssq_done = sem("x1ssq_done")
        h2_done = sem("h2_done")
        part_done = [sem(f"part_done{i}") for i in range(3)]
        rest_scaled = sem("rest_scaled")
        rest_done = [sem(f"rest_done{i}") for i in range(2)]
        x1_stored = sem("x1_stored")
        h2_stored = sem("h2_stored")
        parts_stored = sem("parts_stored")
        state_stored = sem("state_stored")
        x1_left, h2_left, parts_left = sem("x1_left"), sem("h2_left"), sem("parts_left")
        act_own = sem("act_own")
        sp_noted = sem("mix_sp_noted")
        block = ctx.enter_context(nc.Block())

        x_rows = t["x_prompt"][0]

        def store(sp, h, b):
            row = h * HALF + b * P
            sp.wait_ge(x1_done, 1 + 4 * h + b + 1)
            sp.dma_start(scratch["x1"][ds(row, P), :], x1w[:, :]).then_inc(x1_stored, 16)
            sp.wait_ge(h2_done, 4 * h + b + 1)
            sp.dma_start(scratch["h2"][ds(row, P), :], h2w[:, :]).then_inc(h2_stored, 16)
            for n in range(3):
                wait_apart(sp, sp_noted, (part_done[n], 1 + 4 * h + b + 1))
                sp.dma_start(scratch["h2_parts"][n, ds(row, P), :], parts[:, n, :]).then_inc(parts_stored, 16)
            sp.wait_ge(x1_stored, 64 * h + 16 * b + 16)
            sp.sem_inc(x1_left, 1)
            sp.wait_ge(h2_stored, 64 * h + 16 * b + 16)
            sp.sem_inc(h2_left, 1)
            sp.wait_ge(parts_stored, 192 * h + 48 * b + 48)
            sp.sem_inc(parts_left, 1)

        @block.sync
        def _(sp):
            mod = scratch["mod"]
            with nc.allow_non_contiguous_dma("feature-major vectors"):
                sp.dma_start(scale1_f[:, :], mod[NS, SCALE1, :].rearrange("(k p) -> p k", p=P)).then_inc(mods_landed, 16)
                sp.dma_start(shift1_f[:, :], mod[NS, SHIFT1, :].rearrange("(k p) -> p k", p=P)).then_inc(mods_landed, 16)
                sp.dma_start(conv_w[:, :, :], t["conv_w"][0].rearrange("(c p) k -> p c k", p=P)).then_inc(mods_landed, 16)
            for dst, n in ((gate1_b, GATE1), (scale2_b, SCALE2), (shift2_b, SHIFT2)):
                sp.dma_start(dst[:, :], mod[NS:NS + 1, n, :].to_broadcast([P, D])).then_inc(mods_landed, 16)
            sp.dma_start(v_gain[:, :], t["sgu_norm_g"][0:1, :].to_broadcast([P, CONV])).then_inc(mods_landed, 16)
            sp.dma_start(bs_row[:, :], t["b_s"].rearrange("a g t -> a (g t)")).then_inc(mods_landed, 16)

            for primed in (x1_left, h2_left, parts_left):
                sp.sem_inc(primed, 1)
            with sp.Fori(0, 2) as h:
                for b in range(TB):
                    i = b % 2
                    if b >= 2:
                        sp.wait_ge(xn_done, 1 + 4 * h + b - 1)
                    else:
                        sp.wait_ge(x1_done, 1 + 4 * h)
                    sp.dma_start(x_in[i][:, :], x_rows[ds(h * HALF + b * P, P), :]).then_inc(x_landed[i], 16)
                for b in range(TB):
                    i = b % 2
                    if b < 2:
                        sp.wait_ge(xn_done, 1 + 4 * h + 4)
                    else:
                        sp.wait_ge(x1_done, 1 + 4 * h + b - 1)
                    sp.dma_start(x_in[i][:, :], x_rows[ds(h * HALF + b * P, P), :]).then_inc(xr_landed[i], 16)
                    if b >= 1:
                        store(sp, h, b - 1)
                store(sp, h, TB - 1)
            sp.wait_ge(tail_moved, 1 + 2)
            with nc.allow_non_contiguous_dma("conv state, feature-major"):
                for c in range(CB):
                    sp.dma_start(t["new_conv_prompt"][0, 0, :, c * P:(c + 1) * P].rearrange("k p -> p k"),
                                 z[:, c, 0:2]).then_inc(state_stored, 16)
            sp.wait_ge(state_stored, 16 * CB)
            sp.wait_ge(x1_stored, 16 * 8)
            sp.wait_ge(h2_stored, 16 * 8)
            sp.wait_ge(parts_stored, 48 * 8)

        @block.gpsimd
        def _(pool):
            pool.memset(ones_row[:, :], 1.0).then_inc(const_done, 1)
            pool.memset(eps[:, :], EPS).then_inc(const_done, 1)
            pool.memset(z[:, :, 0:2], 0.0).then_inc(const_done, 1)

        @block.scalar
        def _(act):
            act.dma_start(w_out[:, :, :], t["w_out"][0].rearrange("(k p) n -> p k n", p=P)).then_inc(weights_landed, 16)
            for primed in (mixed_kept, *part_done):
                act.sem_inc(primed, 1)
            act.wait_ge(const_done, 3)
            act.wait_ge(mods_landed, 16 * 8)

            def std(src, width, done, base, acc):
                nc.scalar.activation(junk[:, 0:width], src, ACT.Square, accum_out=stat[:, acc, 0:1]).then_inc(act_own, 1)
                act.wait_ge(act_own, base)
                nc.scalar.activation(stat[:, acc, 1:2], stat[:, acc, 0:1], ACT.Sqrt, scale=1.0 / D,
                                     bias=eps[:, 0:1]).then_inc(done, 1)

            with act.Fori(0, 2) as h:
                for b in range(TB + 1):
                    if b < TB:
                        act.wait_ge(x_landed[b % 2], 32 * h + 16 * (b // 2) + 16)
                        act.wait_ge(dve_x, 1 + 4 * h + b)
                        std(x_in[b % 2][:, :], D, ssq_done, 12 * h + b + 1, 0)
                    if b >= 1:
                        c = b - 1
                        act.wait_ge(xT_done, 4 * h + c + 1)
                        for k in range(KD):
                            last = nc.scalar.activation(hT[:, k, c * P:(c + 1) * P], pair[c % 2][:, k * P:(k + 1) * P],
                                                        ACT.Identity, scale=scale1_f[:, k:k + 1],
                                                        bias=shift1_f[:, k:k + 1])
                        last.then_inc(hT_done, 1)
                for b in range(TB + 1):
                    if b < TB:
                        act.wait_ge(var_ready, 4 * h + b + 1)
                        nc.scalar.activation(gstat[:, 3, :], gstat[:, 2, :], ACT.Sqrt, scale=1.0 / P,
                                             bias=eps[:, 0:1]).then_inc(vstd_done, 1)
                    if b >= 1:
                        c = b - 1
                        act.wait_ge(mixed_done, 1 + 4 * h + c + 1)
                        nc.scalar.activation(yT[:, CB:KD, c * P:(c + 1) * P],
                                             ps_mixed[:, :].rearrange("p (g n) -> p g n", g=G), ACT.Copy
                                             ).then_inc(mixed_kept, 1)
                for c in range(CB):
                    act.wait_ge(c_done, 4 * h + c + 1)
                    if c >= 1:
                        act.wait_ge(dve_conv, 16 * h + 4 * (c - 1) + 1)
                    else:
                        act.wait_ge(vn_done, 1 + 4 * h + 4)
                    nc.scalar.activation(c_sb[:, :], ps_c, ACT.Copy).then_inc(c_copied, 1)
                for b in range(TB):
                    act.wait_ge(o_done, 4 * h + b + 1)
                    act.wait_ge(dve_o, 1 + 8 * h + 2 * b)
                    std(ps_o[b % 2][:, :], D, ossq_done, 12 * h + 4 + 2 * b + 1, 1)
                    act.wait_ge(x1_done, 1 + 4 * h + b + 1)
                    std(x1w[:, :], D, x1ssq_done, 12 * h + 4 + 2 * b + 2, 2)
                    act.wait_ge(h2_done, 4 * h + b + 1)
                    act.wait_ge(parts_left, 1 + 4 * h + b)
                    nc.scalar.activation(parts[:, 0, :], h2w[:, :], ACT.Copy).then_inc(part_done[0], 1)
                    for n in range(2):
                        act.wait_ge(rest_done[n], 4 * h + b + 1)
                        nc.scalar.activation(parts[:, n + 1, :], rest[:, :], ACT.Copy).then_inc(part_done[n + 1], 1)

        @block.vector
        def _(dve):
            for primed in (x1_done, dve_x, dve_o, xn_done, tail_moved, o_used, vn_done):
                dve.sem_inc(primed, 1)
            dve.wait_ge(mods_landed, 16 * 8)
            dve.wait_ge(const_done, 3)

            def groups(ap):
                return ap.rearrange("p (g n) -> p g n", g=G)

            def per_group(n):
                return gstat[:, n, :].rearrange("p (g o) -> p g o", o=1).to_broadcast([P, G, P])

            with dve.Fori(0, 2) as h:
                for b in range(TB):
                    dve.wait_ge(ssq_done, 4 * h + b + 1)
                    if b >= 2:
                        dve.wait_ge(xT_done, 4 * h + b - 1)
                    if b == 0:
                        dve.wait_ge(x1_left, 1 + 4 * h)
                        dve.wait_ge(h2_left, 1 + 4 * h)
                    dve.wait_ge(xn_done, 1 + 4 * h + b)
                    dve.reciprocal(stat[:, 0, 2:3], stat[:, 0, 1:2]).then_inc(dve_x, 1)
                    dve.wait_ge(dve_x, 1 + 4 * h + b + 1)
                    dve.tensor_scalar(rows[b % 2][:, :], x_in[b % 2][:, :], stat[:, 0, 2:3], None, ALU.mult
                                      ).then_inc(xn_done, 1)
                for b in range(TB):
                    dve.wait_ge(v_done, 4 * h + b + 1)
                    own = Steps(dve, dve_v, 24 * h + 6 * b)
                    own.did(dve.tensor_reduce(gstat[:, 0, :], groups(ps_v[:, :]), AX, ALU.add))
                    own.settle()
                    own.did(dve.tensor_scalar(gstat[:, 1, :], gstat[:, 0, :], -1.0 / P, None, ALU.mult))
                    own.settle()
                    own.did(dve.tensor_tensor(groups(v_dev[:, :]), groups(ps_v[:, :]), per_group(1), ALU.add))
                    own.settle()
                    own.did(dve.tensor_tensor(v_sq[:, :], v_dev[:, :], v_dev[:, :], ALU.mult))
                    own.settle()
                    dve.tensor_reduce(gstat[:, 2, :], groups(v_sq[:, :]), AX, ALU.add).then_inc(var_ready, 1)
                    dve.wait_ge(vstd_done, 4 * h + b + 1)
                    own.did(dve.reciprocal(gstat[:, 4, :], gstat[:, 3, :]))
                    own.settle()
                    own.did(dve.tensor_tensor(groups(v_dev[:, :]), groups(v_dev[:, :]), per_group(4), ALU.mult))
                    own.settle()
                    dve.wait_ge(mixed_done, 1 + 4 * h + b)
                    dve.tensor_tensor(v_norm[:, :], v_dev[:, :], v_gain[:, :], ALU.mult).then_inc(vn_done, 1)
                dve.wait_ge(tail_moved, 1 + h)
                for c in range(CB):
                    own = Steps(dve, dve_conv, 16 * h + 4 * c)
                    dve.wait_ge(c_copied, 4 * h + c + 1)
                    dve.wait_ge(h_done, 4 * h + c + 1)
                    own.did(dve.tensor_tensor(z[:, c, 2:2 + HALF], c_sb[:, :], ps_h, ALU.mult))
                    own.settle()
                    if c >= 1:
                        dve.wait_ge(conv_done, 4 * h + c)
                    own.did(dve.tensor_scalar(y_sb[:, :], z[:, c, 0:HALF], conv_w[:, c, 0:1], None, ALU.mult))
                    for k in (1, 2):
                        own.settle()
                        own.did(dve.scalar_tensor_tensor(out=y_sb[:, :], in0=z[:, c, k:k + HALF],
                                                         scalar=conv_w[:, c, k:k + 1], in1=y_sb[:, :],
                                                         op0=ALU.mult, op1=ALU.add))
                    own.settle()
                    dve.wait_ge(b_done, 4 * h + c + 1)
                    dve.tensor_tensor(yT[:, c, :], y_sb[:, :], ps_b, ALU.mult).then_inc(conv_done, 1)
                dve.tensor_copy(z[:, :, 0:2], z[:, :, HALF:HALF + 2]).then_inc(tail_moved, 1)
                for g in range(G):
                    dve.wait_ge(mixed_kept, 1 + 4 * h + 4)
                    dve.wait_ge(u_done, 4 * h + g + 1)
                    dve.tensor_tensor(yT[:, CB + g, :], yT[:, CB + g, :], ps_u[g % 2], ALU.mult
                                      ).then_inc(gated_done, 1)
                for b in range(TB):
                    own = Steps(dve, dve_o, 1 + 8 * h + 2 * b)
                    dve.wait_ge(ossq_done, 4 * h + b + 1)
                    own.did(dve.reciprocal(stat[:, 1, 2:3], stat[:, 1, 1:2]))
                    own.settle()
                    dve.wait_ge(x1_left, 1 + 4 * h + b)
                    dve.scalar_tensor_tensor(out=x1w[:, :], in0=ps_o[b % 2][:, :], scalar=stat[:, 1, 2:3],
                                             in1=gate1_b[:, :], op0=ALU.mult, op1=ALU.mult).then_inc(o_used, 1)
                    dve.wait_ge(o_used, 1 + 4 * h + b + 1)
                    dve.wait_ge(xr_landed[b % 2], 32 * h + 16 * (b // 2) + 16)
                    dve.tensor_tensor(x1w[:, :], x1w[:, :], x_in[b % 2][:, :], ALU.add).then_inc(x1_done, 1)
                    dve.wait_ge(x1ssq_done, 4 * h + b + 1)
                    own.did(dve.reciprocal(stat[:, 2, 2:3], stat[:, 2, 1:2]))
                    own.settle()
                    dve.wait_ge(h2_left, 1 + 4 * h + b)
                    dve.wait_ge(part_done[2], 1 + 4 * h + b)
                    dve.scalar_tensor_tensor(out=rest[:, :], in0=x1w[:, :], scalar=stat[:, 2, 2:3],
                                             in1=scale2_b[:, :], op0=ALU.mult, op1=ALU.mult).then_inc(rest_scaled, 1)
                    dve.wait_ge(rest_scaled, 4 * h + b + 1)
                    dve.tensor_tensor(h2w[:, :], rest[:, :], shift2_b[:, :], ALU.add).then_inc(h2_done, 1)
                    for n, src in ((0, h2w), (1, rest)):
                        if n == 0:
                            dve.wait_ge(h2_done, 4 * h + b + 1)
                        dve.wait_ge(part_done[n], 1 + 4 * h + b + 1)
                        dve.tensor_tensor(rest[:, :], src[:, :], parts[:, n, :], ALU.subtract
                                          ).then_inc(rest_done[n], 1)

        @block.tensor
        def _(pe):
            pe.sem_inc(mixed_done, 1)
            def project(out, col, h=None):
                for k in range(KD):
                    last = pe.matmul(out, w_in[:, k, col:col + P], hT[:, k, :], start=(k == 0), stop=(k == KD - 1))
                return last

            with pe.Fori(0, 2) as h:
                for b in range(TB):
                    pe.wait_ge(xn_done, 1 + 4 * h + b + 1)
                    if b >= 2:
                        pe.wait_ge(hT_done, 4 * h + b - 1)
                    else:
                        pe.wait_ge(o_used, 1 + 4 * h)
                    for k in range(KD):
                        last = pe.transpose(pair[b % 2][:, k * P:(k + 1) * P], rows[b % 2][:, k * P:(k + 1) * P],
                                            ident[:, :])
                    last.then_inc(xT_done, 1)
                for b in range(TB + 1):
                    if b < TB:
                        pe.wait_ge(hT_done, 4 * h + b + 1)
                        pe.wait_ge(vn_done, 1 + 4 * h + b)
                        for k in range(KD):
                            last = pe.matmul(ps_v[:, :], hT[:, k, b * P:(b + 1) * P],
                                             w_in[:, k, 3 * CONV + CONV:IN_DIM], start=(k == 0), stop=(k == KD - 1))
                        last.then_inc(v_done, 1)
                    if b >= 1:
                        pe.wait_ge(vn_done, 1 + 4 * h + b)
                        pe.wait_ge(mixed_kept, 1 + 4 * h + b - 1)
                        for g in range(G):
                            pe.matmul(ps_mixed[:, g * P:(g + 1) * P], v_norm[:, g * P:(g + 1) * P], wsT[:, g, :],
                                      start=True, stop=False)
                            last = pe.matmul(ps_mixed[:, g * P:(g + 1) * P], ones_row[:, :],
                                             bs_row[:, g * P:(g + 1) * P], start=False, stop=True)
                        last.then_inc(mixed_done, 1)
                for c in range(CB):
                    if c >= 1:
                        pe.wait_ge(c_copied, 4 * h + c)
                    project(ps_c, CONV + c * P).then_inc(c_done, 1)
                    if c >= 1:
                        pe.wait_ge(dve_conv, 16 * h + 4 * (c - 1) + 1)
                    project(ps_h, 2 * CONV + c * P).then_inc(h_done, 1)
                    if c >= 1:
                        pe.wait_ge(conv_done, 4 * h + c)
                    project(ps_b, c * P).then_inc(b_done, 1)
                for g in range(G):
                    if g >= 2:
                        pe.wait_ge(gated_done, 4 * h + g - 1)
                    project(ps_u[g % 2], 3 * CONV + g * P).then_inc(u_done, 1)
                pe.wait_ge(weights_landed, 16)
                pe.wait_ge(gated_done, 4 * h + 4)
                pe.wait_ge(conv_done, 4 * h + 4)
                for b in range(TB):
                    if b >= 2:
                        pe.wait_ge(o_used, 1 + 4 * h + b - 1)
                    for n in range(2):
                        for k in range(KD):
                            last = pe.matmul(ps_o[b % 2][:, n * HALF:(n + 1) * HALF], yT[:, k, b * P:(b + 1) * P],
                                             w_out[:, k, n * HALF:(n + 1) * HALF], start=(k == 0), stop=(k == KD - 1))
                    last.then_inc(o_done, 1)


def mix_sample(nc, t, scratch, ident, w_in):
    with ExitStack() as ctx:
        def sb(name, shape, dt=F32):
            return ctx.enter_context(nc.sbuf_tensor(name, shape, dt))

        def sem(name):
            return ctx.enter_context(nc.semaphore(name))

        w_out = sb("ws_out", [P, KD, D])
        mod = sb("s_mod", [NS, 6, D])
        x = sb("s_x", [NS, D])
        h = sb("s_h", [NS, D])
        y = sb("s_y", [NS, D])
        x1 = sb("s_x1", [NS, D])
        h2 = sb("s_h2", [NS, D])
        junk = sb("s_junk", [NS, D])
        rest = junk
        parts = sb("s_parts", [NS, 3, D], BF16)
        zero = sb("s_zero", [P, D])
        hT = sb("s_hT", [P, KD, NS])
        yT = sb("s_yT", [P, KD, NS])
        before = sb("s_before", [NS, 2, CONV])
        conv_w = sb("s_conv_w", [NS, CONV, 3])
        z = sb("s_z", [NS, CONV])
        c_sb = sb("s_c", [NS, CONV])
        v_dev = sb("s_v_dev", [NS, CONV])
        v_gain = sb("s_v_gain", [NS, CONV])
        w00 = sb("s_w00", [NS, G])
        b0 = sb("s_b0", [NS, G])
        gstat = sb("s_gstat", [NS, 5, G])
        stat = sb("s_stat", [NS, 3, 3])
        eps = sb("s_eps", [NS, 1])
        ps_T = ctx.enter_context(nc.psum_tensor("s_ps_T", [P, KD, NS], F32))
        ps_p = [ctx.enter_context(nc.psum_tensor(f"s_ps_p{n}", [NS, CONV], F32)) for n in range(5)]
        ps_o = ctx.enter_context(nc.psum_tensor("s_ps_o", [NS, D], F32))
        ps_b, ps_c, ps_h, ps_u, ps_v = ps_p

        loaded = sem("s_loaded")
        weights_landed = sem("s_weights_landed")
        const_done = sem("s_const_done")
        rms_step = sem("s_rms_step")
        row_step = sem("s_row_step")
        turned = sem("s_turned")
        projected = sem("s_projected")
        summed = sem("s_summed")
        c_copied = sem("s_c_copied")
        extra_step = sem("s_extra_step")
        yT_copied = sem("s_yT_copied")
        part_done = sem("s_part_done")
        zero_stored = sem("s_zero_stored")
        stored = sem("s_stored")
        block = ctx.enter_context(nc.Block())

        def sample_rows(ap):
            return [ap[SEQ + 32 * j:SEQ + 32 * j + 2, :] for j in range(4)]

        SAMPLE_H, SAMPLE_Z, SAMPLE_VAR, SAMPLE_V, SAMPLE_Y, SAMPLE_X1, SAMPLE_H2 = 4, 5, 14, 17, 20, 23, 26

        @block.sync
        def _(sp):
            sp.dma_start(x[:, :], t["x_sample"].rearrange("b l d -> (b l) d")).then_inc(loaded, 16)
            sp.dma_start(mod[:, :, :], scratch["mod"][0:NS]).then_inc(loaded, 16)
            sp.dma_start(w_out[:, :, :], t["w_out"][0].rearrange("(k p) n -> p k n", p=P)).then_inc(weights_landed, 16)
            sp.dma_start(before[:, :, :], t["state_conv"][0]).then_inc(loaded, 16)
            sp.dma_start(conv_w[:, :, :].rearrange("p c k -> p (c k)"),
                         t["conv_w"].rearrange("a c k -> a (c k)").to_broadcast([NS, 3 * CONV])).then_inc(loaded, 16)
            sp.dma_start(v_gain[:, :], t["sgu_norm_g"][0:1, :].to_broadcast([NS, CONV])).then_inc(loaded, 16)
            with nc.allow_non_contiguous_dma("first position of each group"):
                sp.dma_start(w00[:, :], t["w_s"][0:1, :, 0, 0].to_broadcast([NS, G])).then_inc(loaded, 16)
                sp.dma_start(b0[:, :], t["b_s"][0:1, :, 0].to_broadcast([NS, G])).then_inc(loaded, 16)
            sp.wait_ge(const_done, 2)
            sp.dma_start(scratch["h2"][SEQ:SEQ + P, :], zero[:, :]).then_inc(zero_stored, 16)
            for n in range(3):
                sp.dma_start(scratch["h2_parts"][n, SEQ:SEQ + P, :], zero[:, 0:D // 2].bitcast(BF16)
                             ).then_inc(zero_stored, 16)
            sp.wait_ge(zero_stored, 64)
            sp.wait_ge(row_step, SAMPLE_Z)
            sp.dma_start(t["new_conv_sample"][0, :, 0, :], before[:, 1, :]).then_inc(stored, 16)
            sp.dma_start(t["new_conv_sample"][0, :, 1, :], z[:, :]).then_inc(stored, 16)
            sp.wait_ge(row_step, SAMPLE_V)
            sp.dma_start(t["sgu_v_sample"][0, :, 0, :], v_dev[:, :]).then_inc(stored, 16)
            sp.wait_ge(row_step, SAMPLE_H2)
            for src, dst in ((x1, scratch["x1"]), (h2, scratch["h2"])):
                for j, rows in enumerate(sample_rows(dst)):
                    sp.dma_start(rows, src[2 * j:2 * j + 2, :]).then_inc(stored, 16)
            for n in range(3):
                sp.wait_ge(part_done, n + 1)
                for j, rows in enumerate(sample_rows(scratch["h2_parts"][n])):
                    sp.dma_start(rows, parts[2 * j:2 * j + 2, n, :]).then_inc(stored, 16)
            sp.wait_ge(stored, 16 * (3 + 8 + 12))

        @block.gpsimd
        def _(pool):
            pool.memset(eps[:, :], EPS).then_inc(const_done, 1)
            pool.memset(zero[:, :], 0.0).then_inc(const_done, 1)

        @block.scalar
        def _(act):
            step = Steps(act, rms_step)

            def root(src, acc):
                step.did(nc.scalar.activation(junk[:, :], src, ACT.Square, accum_out=stat[:, acc, 0:1]))
                step.settle()
                step.did(nc.scalar.activation(stat[:, acc, 1:2], stat[:, acc, 0:1], ACT.Sqrt, scale=1.0 / D,
                                              bias=eps[:, 0:1]))

            act.wait_ge(const_done, 1)
            act.wait_ge(loaded, 16 * 7)
            root(x[:, :], 0)
            act.wait_ge(projected, 2)
            nc.scalar.activation(c_sb[:, :], ps_c[:, :], ACT.Copy).then_inc(c_copied, 1)
            act.wait_ge(row_step, SAMPLE_VAR)
            step.did(nc.scalar.activation(gstat[:, 3, :], gstat[:, 2, :], ACT.Sqrt, scale=1.0 / P, bias=eps[:, 0:1]))
            act.wait_ge(summed, 1)
            root(ps_o[:, :], 1)
            act.wait_ge(row_step, SAMPLE_X1)
            root(x1[:, :], 2)
            act.wait_ge(row_step, SAMPLE_H2)
            for n in range(3):
                if n:
                    act.wait_ge(row_step, SAMPLE_H2 + n)
                nc.scalar.activation(parts[:, n, :], (rest if n else h2)[:, :], ACT.Copy).then_inc(part_done, 1)

        @block.vector
        def _(dve):
            own = Steps(dve, row_step)

            def do(ins):
                own.did(ins)
                own.settle()

            def groups(ap):
                return ap.rearrange("p (g n) -> p g n", g=G)

            def per_group(ap):
                return ap.rearrange("p (g o) -> p g o", o=1).to_broadcast([NS, G, P])

            dve.wait_ge(loaded, 16 * 7)
            dve.wait_ge(rms_step, 2)
            do(dve.reciprocal(stat[:, 0, 2:3], stat[:, 0, 1:2]))
            do(dve.scalar_tensor_tensor(out=h[:, :], in0=x[:, :], scalar=stat[:, 0, 2:3], in1=mod[:, SCALE1, :],
                                        op0=ALU.mult, op1=ALU.mult))
            do(dve.tensor_tensor(h[:, :], h[:, :], mod[:, SHIFT1, :], ALU.add))
            dve.wait_ge(turned, 1)
            do(dve.tensor_copy(hT[:, :, :], ps_T[:, :, :]))
            assert own.n == SAMPLE_H
            dve.wait_ge(c_copied, 1)
            dve.wait_ge(projected, 3)
            do(dve.tensor_tensor(z[:, :], c_sb[:, :], ps_h[:, :], ALU.mult))
            assert own.n == SAMPLE_Z
            do(dve.tensor_tensor(y[:, 0:CONV], before[:, 0, :], conv_w[:, :, 0], ALU.mult))
            do(dve.tensor_tensor(c_sb[:, :], before[:, 1, :], conv_w[:, :, 1], ALU.mult))
            do(dve.tensor_tensor(y[:, 0:CONV], y[:, 0:CONV], c_sb[:, :], ALU.add))
            do(dve.tensor_tensor(c_sb[:, :], z[:, :], conv_w[:, :, 2], ALU.mult))
            do(dve.tensor_tensor(y[:, 0:CONV], y[:, 0:CONV], c_sb[:, :], ALU.add))
            dve.wait_ge(projected, 5)
            do(dve.tensor_reduce(gstat[:, 0, :], groups(ps_v[:, :]), AX, ALU.add))
            do(dve.tensor_scalar(gstat[:, 1, :], gstat[:, 0, :], -1.0 / P, None, ALU.mult))
            do(dve.tensor_tensor(groups(v_dev[:, :]), groups(ps_v[:, :]), per_group(gstat[:, 1, :]), ALU.add))
            dve.tensor_tensor(c_sb[:, :], v_dev[:, :], v_dev[:, :], ALU.mult).then_inc(extra_step, 1)
            dve.wait_ge(extra_step, 1)
            do(dve.tensor_reduce(gstat[:, 2, :], groups(c_sb[:, :]), AX, ALU.add))
            assert own.n == SAMPLE_VAR
            dve.wait_ge(rms_step, 3)
            do(dve.reciprocal(gstat[:, 4, :], gstat[:, 3, :]))
            do(dve.tensor_tensor(groups(v_dev[:, :]), groups(v_dev[:, :]), per_group(gstat[:, 4, :]), ALU.mult))
            do(dve.tensor_tensor(v_dev[:, :], v_dev[:, :], v_gain[:, :], ALU.mult))
            assert own.n == SAMPLE_V
            do(dve.tensor_tensor(groups(c_sb[:, :]), groups(v_dev[:, :]), per_group(w00[:, :]), ALU.mult))
            do(dve.tensor_tensor(groups(c_sb[:, :]), groups(c_sb[:, :]), per_group(b0[:, :]), ALU.add))
            dve.tensor_tensor(y[:, 0:CONV], y[:, 0:CONV], ps_b[:, :], ALU.mult).then_inc(extra_step, 1)
            dve.wait_ge(extra_step, 2)
            do(dve.tensor_tensor(y[:, CONV:D], c_sb[:, :], ps_u[:, :], ALU.mult))
            assert own.n == SAMPLE_Y
            dve.wait_ge(turned, 2)
            dve.tensor_copy(yT[:, :, :], ps_T[:, :, :]).then_inc(yT_copied, 1)
            dve.wait_ge(rms_step, 5)
            do(dve.reciprocal(stat[:, 1, 2:3], stat[:, 1, 1:2]))
            do(dve.scalar_tensor_tensor(out=x1[:, :], in0=ps_o[:, :], scalar=stat[:, 1, 2:3], in1=mod[:, GATE1, :],
                                        op0=ALU.mult, op1=ALU.mult))
            do(dve.tensor_tensor(x1[:, :], x1[:, :], x[:, :], ALU.add))
            assert own.n == SAMPLE_X1
            dve.wait_ge(rms_step, 7)
            do(dve.reciprocal(stat[:, 2, 2:3], stat[:, 2, 1:2]))
            do(dve.scalar_tensor_tensor(out=h2[:, :], in0=x1[:, :], scalar=stat[:, 2, 2:3], in1=mod[:, SCALE2, :],
                                        op0=ALU.mult, op1=ALU.mult))
            do(dve.tensor_tensor(h2[:, :], h2[:, :], mod[:, SHIFT2, :], ALU.add))
            assert own.n == SAMPLE_H2
            for n in range(2):
                dve.wait_ge(part_done, n + 1)
                do(dve.tensor_tensor(rest[:, :], (rest if n else h2)[:, :], parts[:, n, :], ALU.subtract))

        @block.tensor
        def _(pe):
            pe.wait_ge(row_step, SAMPLE_H - 1)
            for k in range(KD):
                last = pe.transpose(ps_T[:, k, :], h[:, k * P:(k + 1) * P], ident[0:NS, 0:NS])
            last.then_inc(turned, 1)
            pe.wait_ge(row_step, SAMPLE_H)
            for n in range(5):
                for k in range(KD):
                    last = pe.matmul(ps_p[n][:, :], hT[:, k, :], w_in[:, k, n * CONV:(n + 1) * CONV],
                                     start=(k == 0), stop=(k == KD - 1))
                last.then_inc(projected, 1)
            pe.wait_ge(row_step, SAMPLE_Y)
            for k in range(KD):
                last = pe.transpose(ps_T[:, k, :], y[:, k * P:(k + 1) * P], ident[0:NS, 0:NS])
            last.then_inc(turned, 1)
            pe.wait_ge(yT_copied, 1)
            pe.wait_ge(weights_landed, 16)
            for n in range(2):
                for k in range(KD):
                    last = pe.matmul(ps_o[:, n * HALF:(n + 1) * HALF], yT[:, k, :],
                                     w_out[:, k, n * HALF:(n + 1) * HALF], start=(k == 0), stop=(k == KD - 1))
            last.then_inc(summed, 1)


def peer(nc, t, scratch, ident):
    RING = 8
    BODY = 8
    QCOLS = 2 * KEYS
    CAND = TOPK * TOPK
    CHAIN = 25
    PAIRS = HEADS - 2
    with ExitStack() as ctx:
        def sb(name, shape, dt=F32):
            return ctx.enter_context(nc.sbuf_tensor(name, shape, dt))

        def sem(name):
            return ctx.enter_context(nc.semaphore(name))

        w_q = sb("w_q", [P, KD, HEADS * QCOLS])
        keysT = sb("keysT", [P, HEADS * 2, KEYS])
        h2_in = sb("h2_in", [P, D])
        h2T = sb("h2T", [P, KD, P])
        h2_bf = sb("h2_bf", [96, 2, 4, D], BF16)
        u_rows = [sb(f"u_rows{s}", [P, D]) for s in range(RING)]
        v_rows = [sb(f"v_rows{s}", [P, D]) for s in range(RING)]
        q_sb = sb("q_sb", [P, QCOLS])
        qT_sb = sb("qT_sb", [P, QCOLS])
        s_sb = sb("s_sb", [P, 2, KEYS])
        s_less = sb("s_less", [P, 2, KEYS])
        top_v = sb("top_v", [P, 2, TOPK])
        top_i = sb("top_i", [P, 2, TOPK], U32)
        top_f = sb("top_f", [P, 2, TOPK])
        cand = sb("cand", [P, TOPK, TOPK])
        cand_less = sb("cand_less", [P, CAND])
        pair_v = sb("pair_v", [P, TOPK])
        pair_i = sb("pair_i", [P, TOPK], U32)
        pair_hl = sb("pair_hl", [P, 2, TOPK], U32)
        pair_f = sb("pair_f", [P, 2, TOPK])
        pick = sb("pick", [P, 2, TOPK, TOPK])
        pick_f = sb("pick_f", [P, 2, TOPK])
        count_i = sb("count_i", [P, TOPK], mybir.dt.int32)
        count = sb("count", [P, TOPK])
        expert_f = sb("expert_f", [P, HEADS * TOPK])
        best = sb("best", [P, HEADS, TOPK])
        gate = sb("gate", [P, HEADS, TOPK])
        total = sb("total", [P, HEADS])
        inverse = sb("inverse", [P, HEADS])
        expertT = sb("expertT", [P, NBLK, 4, 32], U32)
        gateT = sb("gateT", [P, NBLK, 4, 32])
        u_idx = [sb(f"u_idx{i}", [P, BODY], U32) for i in range(2)]
        v_idx = [sb(f"v_idx{i}", [P, BODY], U32) for i in range(2)]
        dot = [sb(f"dot{i}", [P, 4]) for i in range(2)]
        act_u = [sb(f"act_u{i}", [P, 4]) for i in range(2)]
        weight = [sb(f"weight{s}", [P, 32]) for s in range(BODY)]
        window = sb("window", [P, 63])
        pick_row = sb("pick_row", [96, 32], BF16)
        y_stat = sb("y_stat", [P, 3])
        eps = sb("p_eps", [P, 1])
        x1_in = sb("x1_in", [P, D])
        out_rows = sb("out_rows", [P, D])
        gate2_b = sb("gate2_b", [P, D])
        gate2_s = sb("gate2_s", [P, D])
        zeros = sb("zeros", [P, HALF], BF16)
        gain2 = v_rows[0]

        ps_x = [ctx.enter_context(nc.psum_tensor(f"ps_x{i}", [P, D], F32)) for i in range(2)]
        ps_y = ctx.enter_context(nc.psum_tensor("ps_y", [P, D], F32))
        ps_a = ctx.enter_context(nc.psum_tensor("ps_a", [P, 4, P], F32))
        ps_b = ctx.enter_context(nc.psum_tensor("ps_b2", [P, 4, P], F32))
        flat_a = ps_a[:, :, :].rearrange("p a b -> p (a b)")
        flat_b = ps_b[:, :, :].rearrange("p a b -> p (a b)")

        wq_landed = sem("wq_landed")
        keys_landed = [sem(f"keys_landed{i}") for i in range(2)]
        gains_landed = sem("p_gains_landed")
        h2_landed = sem("h2_landed")
        bf_landed = sem("bf_landed")
        x1_landed = sem("x1_landed")
        u_landed = [sem(f"u_landed{s}") for s in range(RING)]
        v_landed = [sem(f"v_landed{s}") for s in range(RING)]
        v_used = [sem(f"v_used{s}") for s in range(RING)]
        const_done = sem("p_const_done")
        sp_noted, act_noted = sem("sp_noted"), sem("act_noted")
        dve_noted, pool_noted = sem("dve_noted"), sem("pool_noted")
        keys_turned = sem("keys_turned")
        keys_copied = sem("keys_copied")
        gate2_done = sem("gate2_done")
        h2_turned = sem("h2_turned")
        h2T_done = sem("h2T_done")
        q_done = sem("q_done")
        q_copied = sem("q_copied")
        qT_done = sem("qT_done")
        qT_copied = sem("qT_copied")
        s_done = sem("s_done")
        s_copied = sem("s_copied")
        head_step = sem("head_step")
        soft_step = sem("soft_step")
        exp_done = sem("exp_done")
        picked_turned = sem("picked_turned")
        expert_ready = sem("expert_ready")
        gate_ready = sem("gate_ready")
        u_idx_ready = sem("u_idx_ready")
        v_idx_ready = sem("v_idx_ready")
        x_spread = sem("x_spread")
        dots_done = sem("dots_done")
        gelu_done = sem("gelu_done")
        weight_done = sem("weight_done")
        y_done = sem("y_done")
        y_ssq = sem("y_ssq")
        y_std = sem("y_std")
        y_inverse = sem("y_inverse")
        y_used = sem("y_used")
        out_done = sem("out_done")
        out_stored = sem("out_stored")
        out_left = sem("out_left")
        block = ctx.enter_context(nc.Block())

        def load_rows(sp, blk):
            wait_apart(sp, sp_noted, (h2_turned, 2 * blk))
            sp.dma_start(h2_in[:, :], scratch["h2"][ds(blk * P, P), :]).then_inc(h2_landed, 16)

        def load_parts(sp, blk):
            wait_apart(sp, sp_noted, (dots_done, 1 + P * (blk - 1)))
            for n in range(3):
                sp.dma_start(h2_bf[32 * n:32 * n + 32, ds(blk % 2, 1), :, :].rearrange("p a j d -> p (a j) d"),
                             scratch["h2_parts"][n, ds(blk * P, P), :].rearrange("(j i) d -> i j d", i=32)
                             ).then_inc(bf_landed, 16)

        @block.sync
        def _(sp):
            sp.sem_inc(out_left, 1)
            sp.dma_start(h2_in[:, :], scratch["h2"][0:P, :]).then_inc(h2_landed, 16)
            sp.dma_start(w_q[:, :, 0:HEADS * KEYS],
                         t["w_q"][0].rearrange("(k p) n -> p k n", p=P)[:, :, 0:HEADS * KEYS]).then_inc(wq_landed, 16)
            for n in range(3):
                sp.dma_start(h2_bf[32 * n:32 * n + 32, 0, :, :],
                             scratch["h2_parts"][n, 0:P, :].rearrange("(j i) d -> i j d", i=32)).then_inc(bf_landed, 16)
            sp.dma_start(w_q[:, :, HEADS * KEYS:],
                         t["w_q"][0].rearrange("(k p) n -> p k n", p=P)[:, :, HEADS * KEYS:]).then_inc(wq_landed, 16)
            load_rows(sp, 1)
            load_parts(sp, 1)

            def rows_of(b, more):
                if more:
                    load_rows(sp, b + 2)
                sp.wait_ge(out_done, 1 + b)
                sp.dma_start(x1_in[:, :], scratch["x1"][ds(b * P, P), :]).then_inc(x1_landed, 16)
                if more:
                    load_parts(sp, b + 2)
                sp.wait_ge(out_done, 1 + b + 1)
                sp.dma_start(t["y_prompt"][0, ds(b * P, P), :], out_rows[:, :]).then_inc(out_stored, 16)
                sp.wait_ge(out_stored, 16 * b + 16)
                sp.sem_inc(out_left, 1)

            with sp.Fori(0, NBLK - 2) as b:
                rows_of(b, True)
            rows_of(NBLK - 2, False)
            for j in range(4):
                sp.dma_start(x1_in[32 * j:32 * j + 2, :], scratch["x1"][SEQ + 32 * j:SEQ + 32 * j + 2, :]
                             ).then_inc(x1_landed, 16)
            sp.wait_ge(out_done, 1 + NBLK)
            for j in range(4):
                sp.dma_start(t["y_sample"][2 * j:2 * j + 2, 0, :], out_rows[32 * j:32 * j + 2, :]).then_inc(out_stored, 16)
            sp.wait_ge(out_stored, 16 * (NBLK - 1 + 4))

        def gather(pool, rows, table, idx, s, landed):
            pool.indirect_dma_start(rows[s][:, :], None, table[0],
                                    bass.IndirectOffsetOnAxis(ap=idx[:, s:s + 1], axis=0)).then_inc(landed[s], 16)

        @block.gpsimd
        def _(pool):
            pool.memset(window[:, :], 0.0).then_inc(const_done, 1)
            pool.memset(pick_row[:, :], 0.0).then_inc(const_done, 1)
            pool.memset(eps[:, :], EPS).then_inc(const_done, 1)
            pool.iota(count_i[:, :], pattern=[[1, TOPK]], base=0, channel_multiplier=0).then_inc(const_done, 1)
            pool.memset(zeros[:, :], 0.0).then_inc(const_done, 1)
            pool.memset(gate2_s[:, :], 0.0).then_inc(const_done, 1)
            pool.wait_ge(const_done, 6)
            pool.memset(window[:, 31:32], 1.0).then_inc(const_done, 1)
            for n in range(3):
                pool.affine_select(out=pick_row[:, :], in_=pick_row[:, :], compare_op=ALU.not_equal, fill=1.0,
                                   base=-32 * n, pattern=[[-1, 32]], channel_multiplier=1).then_inc(const_done, 1)
                pool.wait_ge(const_done, 8 + n)

            def step(n, par, more):
                waits = [(v_idx_ready, n + 1)] + [(u_idx_ready, n + 2)] * more
                for s in range(BODY):
                    wait_apart(pool, pool_noted, (v_used[s], 1 + n), *waits)
                    waits = []
                    gather(pool, v_rows, t["expert_v"], v_idx[par], s, v_landed)
                    if more:
                        wait_apart(pool, pool_noted, (dots_done, 1 + BODY * n + s + 1))
                        gather(pool, u_rows, t["expert_u"], u_idx[1 - par], s, u_landed)

            pool.wait_ge(u_idx_ready, 1)
            for s in range(BODY):
                gather(pool, u_rows, t["expert_u"], u_idx[0], s, u_landed)
            with pool.Fori(0, (NBLK - 1) * HEADS) as m:
                step(2 * m, 0, True)
                step(2 * m + 1, 1, True)
            step((NBLK - 1) * HEADS * 2, 0, False)

        def normalise(act, b):
            act.wait_ge(out_left, 1 + b)
            act.wait_ge(y_done, b + 1)
            nc.scalar.activation(out_rows[:, :], ps_y[:, :], ACT.Square, accum_out=y_stat[:, 0:1]).then_inc(y_ssq, 1)
            act.wait_ge(y_ssq, b + 1)
            nc.scalar.activation(y_stat[:, 1:2], y_stat[:, 0:1], ACT.Sqrt, scale=1.0 / D, bias=eps[:, 0:1]
                                 ).then_inc(y_std, 1)

        @block.scalar
        def _(act):
            act.sem_inc(s_copied, 1)
            for i in range(2):
                act.dma_start(u_rows[i][:, :].rearrange("k (a c) -> k a c", c=P),
                              t["sub_keys"][0].rearrange("h p k c -> k (h p) c")[:, 8 * i:8 * i + 8, :]
                              ).then_inc(keys_landed[i], 16)
            act.dma_start(gate2_b[:, :], scratch["mod"][NS:NS + 1, GATE2, :].to_broadcast([P, D])).then_inc(gains_landed, 16)
            act.wait_ge(const_done, 10)
            for j in range(4):
                act.dma_start(gate2_s[32 * j:32 * j + 2, :], scratch["mod"][2 * j:2 * j + 2, GATE2, :]
                              ).then_inc(gains_landed, 16)
            act.dma_start(gain2[:, :], t["g_post_ffn"][0:1, :].to_broadcast([P, D])).then_inc(gains_landed, 16)

            def turn(blk):
                for n, ps in enumerate((ps_a, ps_b)):
                    act.wait_ge(h2_turned, 2 * blk + n + 1)
                    nc.scalar.activation(h2T[:, 4 * n:4 * n + 4, :], ps[:, :, :], ACT.Copy).then_inc(h2T_done, 1)

            def keep_q(hd):
                act.wait_ge(q_done, hd + 1)
                nc.scalar.activation(q_sb[:, :], flat_a[:, 0:QCOLS], ACT.Copy).then_inc(q_copied, 1)

            def keep_qT(hd):
                act.wait_ge(qT_done, hd + 1)
                nc.scalar.activation(qT_sb[:, :], flat_b[:, 0:QCOLS], ACT.Copy).then_inc(qT_copied, 1)

            def keep_s(hd):
                act.wait_ge(s_done, hd + 1)
                act.wait_ge(head_step, 1 + CHAIN * hd)
                nc.scalar.activation(s_sb[:, :, :].rearrange("p a b -> p (a b)"), flat_a[:, 0:QCOLS], ACT.Copy
                                     ).then_inc(s_copied, 1)

            def soften(blk):
                act.wait_ge(soft_step, 4 * blk + 1)
                nc.scalar.activation(gate[:, :, :], gate[:, :, :], ACT.Exp).then_inc(exp_done, 1)

            def finish(blk):
                wait_apart(act, act_noted, (picked_turned, blk + 1))
                dst = expertT[:, ds(blk, 1), :, :].rearrange("p a j i -> p (a j i)")
                nc.scalar.activation(dst, flat_b[:, 0:P], ACT.Copy).then_inc(expert_ready, 1)
                dst = gateT[:, ds(blk, 1), :, :].rearrange("p a j i -> p (a j i)")
                nc.scalar.activation(dst, flat_b[:, P:2 * P], ACT.Copy).then_inc(gate_ready, 1)
                wait_apart(act, act_noted, (expert_ready, blk + 1))

            def index(dst, blk, i0, done):
                src = expertT[:, ds(blk, 1), :, ds(i0, 2)].rearrange("p a j i -> p i (a j)")
                nc.scalar.activation(dst[:, :].rearrange("p (i j) -> p i j", i=2), src, ACT.Copy).then_inc(done, 1)

            def gelu(n, g):
                act.wait_ge(dots_done, 1 + BODY * n + 4 * g + 4)
                act.wait_ge(v_used[4 * g + 3], 1 + n)
                nc.scalar.activation(act_u[g][:, :], dot[g][:, :], ACT.Gelu).then_inc(gelu_done, 1)

            def step(n, par, v_next, u_next, head=None, after_head=None, first=None):
                if first is not None:
                    first()
                if head is not None:
                    keep_q(head)
                gelu(n, 0)
                if head is not None:
                    keep_qT(head)
                    keep_s(head)
                if after_head is not None:
                    after_head()
                if v_next is not None:
                    wait_apart(act, act_noted, (v_used[BODY - 1], 1 + n))
                    index(v_idx[1 - par], *v_next, v_idx_ready)
                gelu(n, 1)
                if u_next is not None:
                    index(u_idx[par], *u_next, u_idx_ready)

            turn(0)
            with act.Fori(0, HEADS) as h:
                keep_q(h)
                keep_qT(h)
                keep_s(h)
            soften(0)
            finish(0)
            index(u_idx[0], 0, 0, u_idx_ready)
            index(u_idx[1], 0, 2, u_idx_ready)
            index(v_idx[0], 0, 0, v_idx_ready)
            step(0, 0, (0, 2), (0, 4))
            with act.Fori(0, NBLK - 1) as b:
                turn(b + 1)
                hd = HEADS * (b + 1)
                with act.Fori(0, PAIRS) as h:
                    step(16 * b + 2 * h + 1, 1, (b, 4 * h + 4), (b, 4 * h + 6), head=hd + h)
                    step(16 * b + 2 * h + 2, 0, (b, 4 * h + 6), (b, 4 * h + 8))
                step(16 * b + 13, 1, (b, 28), (b, 30), head=hd + PAIRS)
                step(16 * b + 14, 0, (b, 30), None, head=hd + PAIRS + 1, after_head=lambda: soften(b + 1))

                def first():
                    finish(b + 1)
                    index(u_idx[0], b + 1, 0, u_idx_ready)

                step(16 * b + 15, 1, (b + 1, 0), (b + 1, 2), first=first)
                step(16 * b + 16, 0, (b + 1, 2), (b + 1, 4))
                normalise(act, b)
            normalise(act, NBLK - 1)

        @block.vector
        def _(dve):
            for primed in (out_done, head_step, y_used, dots_done):
                dve.sem_inc(primed, 1)
            def keep(r):
                dve.wait_ge(keys_turned, r + 1)
                dve.tensor_copy(keysT[:, 4 * r:4 * r + 4, :], (ps_a, ps_b)[r % 2][:, :, :]).then_inc(keys_copied, 1)

            for r in range(4):
                keep(r)
            dve.wait_ge(gains_landed, 16 * 6)
            dve.tensor_tensor(gate2_b[:, :], gate2_b[:, :], gain2[:, :], ALU.mult).then_inc(gate2_done, 1)
            dve.tensor_tensor(gate2_s[:, :], gate2_s[:, :], gain2[:, :], ALU.mult).then_inc(gate2_done, 1)
            dve.wait_ge(const_done, 10)
            dve.tensor_copy(count[:, :], count_i[:, :]).then_inc(gate2_done, 1)
            dve.wait_ge(gate2_done, 3)

            def retrieve(hd, blk, h):
                own = Steps(dve, head_step, 1 + CHAIN * hd, dve_noted)
                wait_apart(dve, dve_noted, (s_copied, 1 + hd + 1), (picked_turned, blk))
                for p in range(2):
                    own.did(dve.max(top_v[:, p, 0:8], s_sb[:, p, :]))
                own.settle()
                for p in range(2):
                    own.did(dve.match_replace(s_less[:, p, :], top_v[:, p, 0:8], s_sb[:, p, :], LOWEST))
                for p in range(2):
                    own.did(dve.max_index(top_i[:, p, 0:8], top_v[:, p, 0:8], s_sb[:, p, :]))
                own.settle()
                for p in range(2):
                    own.did(dve.max(top_v[:, p, 8:16], s_less[:, p, :]))
                own.settle()
                for p in range(2):
                    own.did(dve.max_index(top_i[:, p, 8:16], top_v[:, p, 8:16], s_less[:, p, :]))
                own.did(dve.tensor_tensor(
                    cand[:, :, :], top_v[:, 0, :].rearrange("p (a o) -> p a o", o=1).to_broadcast([P, TOPK, TOPK]),
                    top_v[:, 1:2, :].to_broadcast([P, TOPK, TOPK]), ALU.add))
                own.settle()
                own.did(dve.tensor_copy(top_f[:, :, :], top_i[:, :, :]))
                flat = cand[:, :, :].rearrange("p a b -> p (a b)")
                hi, lo = pair_v[:, 0:8], pair_v[:, 8:16]
                own.did(dve.max(hi, flat))
                own.settle()
                own.did(dve.match_replace(cand_less[:, :], hi, flat, LOWEST))
                own.did(dve.max_index(pair_i[:, 0:8], hi, flat))
                own.settle()
                own.did(dve.max(lo, cand_less[:, :]))
                own.settle()
                own.did(dve.max_index(pair_i[:, 8:16], lo, cand_less[:, :]))
                own.did(dve.tensor_copy(best[:, ds(h, 1), :].rearrange("p a k -> p (a k)"), pair_v[:, :]))
                own.settle()
                own.did(dve.tensor_single_scalar(pair_hl[:, 0, :], pair_i[:, :], 4, ALU.logical_shift_right))
                own.did(dve.tensor_single_scalar(pair_hl[:, 1, :], pair_i[:, :], TOPK - 1, ALU.bitwise_and))
                own.settle()
                own.did(dve.tensor_copy(pair_f[:, :, :], pair_hl[:, :, :]))
                own.settle()
                ranks = pick[:, :, :, :].rearrange("p a k r -> p (a k) r")
                own.did(dve.tensor_tensor(
                    ranks, count[:, :].rearrange("p (o r) -> p o r", o=1).to_broadcast([P, 2 * TOPK, TOPK]),
                    pair_f[:, :, :].rearrange("p a (k o) -> p (a k) o", o=1).to_broadcast([P, 2 * TOPK, TOPK]),
                    ALU.is_equal))
                own.settle()
                own.did(dve.tensor_tensor(
                    pick[:, :, :, :], pick[:, :, :, :],
                    top_f[:, :, :].rearrange("p a (o r) -> p a o r", o=1).to_broadcast([P, 2, TOPK, TOPK]), ALU.mult))
                own.settle()
                own.did(dve.tensor_reduce(pick_f[:, :, :].rearrange("p a k -> p (a k)"), ranks, AX, ALU.add))
                own.settle()
                own.did(dve.scalar_tensor_tensor(out=expert_f[:, ds(h * TOPK, TOPK)], in0=pick_f[:, 0, :],
                                                 scalar=float(KEYS), in1=pick_f[:, 1, :], op0=ALU.mult, op1=ALU.add))
                own.settle()
                assert own.n == CHAIN, own.n

            def center(blk):
                own = Steps(dve, soft_step, 4 * blk)
                own.did(dve.tensor_tensor(gate[:, :, :], best[:, :, :], best[:, :, 0:1].to_broadcast([P, HEADS, TOPK]),
                                          ALU.subtract))

            def soften(blk):
                own = Steps(dve, soft_step, 4 * blk + 1)
                dve.wait_ge(exp_done, blk + 1)
                own.did(dve.tensor_reduce(total[:, :], gate[:, :, :], AX, ALU.add))
                own.settle()
                own.did(dve.reciprocal(inverse[:, :], total[:, :]))
                own.settle()
                own.did(dve.tensor_tensor(gate[:, :, :], gate[:, :, :],
                                          inverse[:, :].rearrange("p (h o) -> p h o", o=1).to_broadcast([P, HEADS, TOPK]),
                                          ALU.mult))

            def product(n, s):
                dve.wait_ge(x_spread, BODY * n + s + 1)
                dve.wait_ge(u_landed[s], 16 * n + 16)
                dve.tensor_tensor_reduce(u_rows[s][:, :], u_rows[s][:, :], ps_x[s % 2][:, :], 1.0, 0.0, ALU.mult,
                                         ALU.add, dot[s // 4][:, s % 4:s % 4 + 1]).then_inc(dots_done, 1)

            def weigh(n, blk, i0, g):
                dve.wait_ge(gelu_done, 2 * n + g + 1)
                i = i0 + g
                for j in range(4):
                    s = 4 * g + j
                    dve.wait_ge(v_used[s], 1 + n)
                    scale = gateT[:, ds(blk, 1), j, ds(i, 1)].rearrange("p a i -> p (a i)")
                    dve.tensor_scalar(weight[s][:, :], window[:, ds(31 - i, 32)], act_u[g][:, j:j + 1], scale,
                                      ALU.mult, ALU.mult).then_inc(weight_done, 1)

            def step(n, here, before, head=None, last=False):
                product(n, 0)
                if before is not None:
                    weigh(n - 1, *before, 1)
                for s in (1, 2, 3, 4, 5):
                    product(n, s)
                    if s == 4:
                        weigh(n, *here, 0)
                if head is not None:
                    retrieve(*head)
                if last:
                    center(head[1])
                product(n, 6)
                if last:
                    soften(head[1])
                product(n, 7)

            def emit(b, gate2):
                dve.wait_ge(y_std, b + 1)
                dve.reciprocal(y_stat[:, 2:3], y_stat[:, 1:2]).then_inc(y_inverse, 1)
                dve.wait_ge(y_inverse, b + 1)
                dve.scalar_tensor_tensor(out=out_rows[:, :], in0=ps_y[:, :], scalar=y_stat[:, 2:3], in1=gate2[:, :],
                                         op0=ALU.mult, op1=ALU.mult).then_inc(y_used, 1)
                dve.wait_ge(y_used, 1 + b + 1)
                dve.wait_ge(x1_landed, 16 * b + 16)
                if gate2 is gate2_s:
                    dve.wait_ge(x1_landed, 16 * b + 64)
                dve.tensor_tensor(out_rows[:, :], out_rows[:, :], x1_in[:, :], ALU.add).then_inc(out_done, 1)

            with dve.Fori(0, HEADS) as h:
                retrieve(h, 0, h)
            center(0)
            soften(0)
            dve.wait_ge(gate_ready, 1)
            step(0, (0, 0), None)
            with dve.Fori(0, NBLK - 1) as b:
                hd = HEADS * (b + 1)
                with dve.Fori(0, PAIRS) as h:
                    step(16 * b + 2 * h + 1, (b, 4 * h + 2), (b, 4 * h), head=(hd + h, b + 1, h))
                    step(16 * b + 2 * h + 2, (b, 4 * h + 4), (b, 4 * h + 2))
                step(16 * b + 13, (b, 26), (b, 24), head=(hd + PAIRS, b + 1, PAIRS))
                step(16 * b + 14, (b, 28), (b, 26), head=(hd + PAIRS + 1, b + 1, PAIRS + 1), last=True)
                step(16 * b + 15, (b, 30), (b, 28))
                step(16 * b + 16, (b + 1, 0), (b, 30))
                emit(b, gate2_b)
            weigh(16 * (NBLK - 1), NBLK - 1, 0, 1)
            emit(NBLK - 1, gate2_s)

        @block.tensor
        def _(pe):
            for primed in v_used:
                pe.sem_inc(primed, 1)
            for r in range(4):
                pe.wait_ge(keys_landed[r // 2], 16)
                if r >= 2:
                    pe.wait_ge(keys_copied, r - 1)
                for a in range(4):
                    c = 4 * (r % 2) + a
                    last = pe.transpose((ps_a, ps_b)[r % 2][:, a, :], u_rows[r // 2][:, c * P:(c + 1) * P], ident[:, :])
                last.then_inc(keys_turned, 1)

            def turn(blk):
                pe.wait_ge(h2_landed, 16 * blk + 16)
                for n, ps in enumerate((ps_a, ps_b)):
                    if n == 0:
                        pe.wait_ge(s_copied, 1 + HEADS * blk)
                    else:
                        pe.wait_ge(gate_ready, blk)
                    for k in range(4):
                        last = pe.transpose(ps[:, k, :], h2_in[:, (4 * n + k) * P:(4 * n + k + 1) * P], ident[:, :])
                    last.then_inc(h2_turned, 1)

            def queries(hd, blk, h):
                pe.wait_ge(h2T_done, 2 * blk + 2)
                pe.wait_ge(s_copied, 1 + hd)
                for k in range(KD):
                    last = pe.matmul(flat_a[:, 0:QCOLS], h2T[:, k, :], w_q[:, k, ds(h * QCOLS, QCOLS)],
                                     start=(k == 0), stop=(k == KD - 1))
                last.then_inc(q_done, 1)

            def turn_queries(hd):
                pe.wait_ge(q_copied, hd + 1)
                for p in range(2):
                    last = pe.transpose(flat_b[:, p * P:(p + 1) * P], q_sb[:, p * P:(p + 1) * P], ident[:, :])
                last.then_inc(qT_done, 1)

            def scores(hd, h):
                pe.wait_ge(qT_copied, hd + 1)
                for p in range(2):
                    last = pe.matmul(flat_a[:, p * P:(p + 1) * P], qT_sb[:, p * P:(p + 1) * P],
                                     keysT[:, ds(2 * h + p, 1), :].rearrange("p a k -> p (a k)"), start=True, stop=True)
                last.then_inc(s_done, 1)

            def finish(blk):
                pe.wait_ge(head_step, 1 + CHAIN * HEADS * (blk + 1))
                pe.wait_ge(soft_step, 4 * blk + 4)
                pe.transpose(flat_b[:, 0:P], expert_f[:, :], ident[:, :])
                pe.transpose(flat_b[:, P:2 * P], gate[:, :, :].rearrange("p h k -> p (h k)"), ident[:, :]
                             ).then_inc(picked_turned, 1)

            def spread(n, s, blk, i):
                for c in range(2):
                    src = h2_bf[:, ds(blk % 2, 1), s % 4, c * HALF:(c + 1) * HALF].rearrange("p a d -> p (a d)")
                    last = pe.matmul(ps_x[s % 2][:, c * HALF:(c + 1) * HALF], pick_row[:, ds(i, 1)].to_broadcast([96, P]),
                                     src, start=True, stop=True)
                last.then_inc(x_spread, 1)

            def gather_sum(n, s):
                pe.wait_ge(weight_done, BODY * n + s + 1)
                pe.wait_ge(v_landed[s], 16 * n + 16)
                j = 32 * (s % 4)
                for c in range(2):
                    last = pe.matmul(ps_y[j:j + 32, c * HALF:(c + 1) * HALF], weight[s][:, :],
                                     v_rows[s][:, c * HALF:(c + 1) * HALF], start=False, stop=False,
                                     skip_group_check=True)
                last.then_inc(v_used[s], 1)

            def step(n, here, after, head=None, sums=True, picked=None):
                for s in range(BODY):
                    if sums:
                        gather_sum(n - 1, s)
                    pe.wait_ge(dots_done, 1 + BODY * n + s + 1)
                    if s + 2 < BODY:
                        spread(n, s + 2, here[0], here[1] + (s + 2) // 4)
                    elif after is not None:
                        spread(n + 1, s + 2 - BODY, *after)
                    if picked is not None and s == 0:
                        finish(picked)
                    if head is not None:
                        if s == 0:
                            queries(*head)
                        if s == 3:
                            turn_queries(head[0])
                        if s == 4:
                            scores(head[0], head[2])

            def bound(first):
                for c in range(2):
                    last = pe.matmul(ps_y[:, c * HALF:(c + 1) * HALF], zeros[:, 0:P], zeros[:, :], start=first,
                                     stop=not first, skip_group_check=True)
                return last

            pe.wait_ge(keys_copied, 4)
            turn(0)
            pe.wait_ge(wq_landed, 32)
            with pe.Fori(0, HEADS) as h:
                queries(h, 0, h)
                turn_queries(h)
                scores(h, h)
            finish(0)
            pe.wait_ge(bf_landed, 48)
            pe.wait_ge(const_done, 10)
            spread(0, 0, 0, 0)
            spread(0, 1, 0, 0)
            step(0, (0, 0), (0, 2), sums=False)
            with pe.Fori(0, NBLK - 1) as b:
                turn(b + 1)
                pe.wait_ge(y_used, 1 + b)
                bound(True)
                hd = HEADS * (b + 1)
                with pe.Fori(0, PAIRS) as h:
                    step(16 * b + 2 * h + 1, (b, 4 * h + 2), (b, 4 * h + 4), head=(hd + h, b + 1, h))
                    step(16 * b + 2 * h + 2, (b, 4 * h + 4), (b, 4 * h + 6))
                step(16 * b + 13, (b, 26), (b, 28), head=(hd + PAIRS, b + 1, PAIRS))
                step(16 * b + 14, (b, 28), (b, 30), head=(hd + PAIRS + 1, b + 1, PAIRS + 1))
                pe.wait_ge(bf_landed, 48 * b + 96)
                step(16 * b + 15, (b, 30), (b + 1, 0), picked=b + 1)
                step(16 * b + 16, (b + 1, 0), (b + 1, 2))
                bound(False).then_inc(y_done, 1)
            pe.wait_ge(y_used, 1 + NBLK - 1)
            bound(True)
            for s in range(BODY):
                gather_sum(16 * (NBLK - 1), s)
            bound(False).then_inc(y_done, 1)


_INS = ["x_prompt", "x_sample", "state_conv", "c_prompt", "c_sample", "w_ada", "b_ada", "g_pre_mix", "w_in", "conv_w",
        "sgu_norm_g", "w_s", "b_s", "w_out", "g_post_mix", "g_pre_ffn", "w_q", "sub_keys", "expert_u", "expert_v",
        "g_post_ffn"]
_OUTS = [("y_prompt", (1, SEQ, D)), ("y_sample", (NS, 1, D)), ("new_conv_prompt", (1, 1, 2, CONV)),
         ("new_conv_sample", (1, NS, 2, CONV)), ("sgu_v_sample", (1, NS, 1, CONV))]


def kernel(**inputs):
    import concourse.bacc as _bacc
    from concourse.bass_utils import run_bass_kernel_spmd as _run

    nc = _bacc.Bacc("TRN2", target_bir_lowering=False, num_devices=1)
    arrays, t = {}, {}
    for name in _INS:
        a = np.ascontiguousarray(inputs[name])
        arrays[f"in_{name}_dram"] = a
        t[name] = nc.dram_tensor(f"in_{name}_dram", a.shape, mybir.dt.from_np(a.dtype), kind="ExternalInput").ap()
    for name, shape in _OUTS:
        t[name] = nc.dram_tensor(f"out_{name}_dram", shape, F32, kind="ExternalOutput").ap()
    build(nc, t)
    r = _run(nc, [arrays], core_ids=[0])
    return tuple(r.results[0][f"out_{name}_dram"] for name, _ in _OUTS)
```

```python
import numpy as np
from contextlib import ExitStack

import concourse.bass as bass
from concourse import mybir

F32 = mybir.dt.float32
BF16 = mybir.dt.bfloat16
U32 = mybir.dt.uint32
ALU = mybir.AluOpType
ACT = mybir.ActivationFunctionType
AX = mybir.AxisListType.X
ds = bass.ds

P = 128
D = 1024
KD = D // P
SEQ = 1024
NS = 8
CONV = 512
CB = CONV // P
G = 4
IN_DIM = 3 * CONV + 2 * CONV
HEADS = 8
KEYS = 128
TOPK = 16
QCOLS = 2 * KEYS
HALF = 512
TB = HALF // P
NBLK = SEQ // P + 1
EPS = 1e-6
LOWEST = -3.0e38

SHIFT1, SCALE1, GATE1, SHIFT2, SCALE2, GATE2 = range(6)


def wait_apart(eng, noted, *waits):
    for sem, value in waits:
        eng.wait_ge(sem, value)
    eng.sem_inc(noted, 1)


class Steps:

    def __init__(self, eng, sem, base=0, noted=None):
        self.eng, self.sem, self.base, self.n, self.noted = eng, sem, base, 0, noted

    def did(self, ins):
        ins.then_inc(self.sem, 1)
        self.n += 1
        return ins

    def settle(self, back=0):
        value = self.base + self.n - back
        if self.noted is not None:
            wait_apart(self.eng, self.noted, (self.sem, value))
        else:
            self.eng.wait_ge(self.sem, value)


def build(nc, t):
    scratch = {
        "mod": nc.dram_tensor("mod_rows", (9, 6, D), F32, kind="Internal").ap(),
        "x1": nc.dram_tensor("x1_rows", (NBLK * P, D), F32, kind="Internal").ap(),
        "h2": nc.dram_tensor("h2_rows", (NBLK * P, D), F32, kind="Internal").ap(),
        "h2_parts": nc.dram_tensor("h2_part_rows", (3, NBLK * P, D), BF16, kind="Internal").ap(),
    }
    with ExitStack() as ctx:
        ident = ctx.enter_context(nc.sbuf_tensor("ident", [P, P], F32))
        keysT = ctx.enter_context(nc.sbuf_tensor("keysT", [P, HEADS * 2, KEYS], F32))
        wide = ctx.enter_context(nc.sbuf_tensor("wide", [P, KD * IN_DIM], F32))
        w_in = wide[:, :].rearrange("p (k n) -> p k n", k=KD)
        w_q = wide[:, 0:KD * HEADS * QCOLS].rearrange("p (k n) -> p k n", k=KD)
        spare = [wide[:, a:a + D] for a in range(KD * HEADS * QCOLS, KD * IN_DIM, D)]
        with ExitStack() as weights:
            w_out = weights.enter_context(nc.sbuf_tensor("w_out", [P, KD, D], F32))
            wsT = weights.enter_context(nc.sbuf_tensor("wsT", [P, G, P], F32))
            condition(nc, t, scratch, ident, w_in, w_out, wsT, keysT)
            mix_prompt(nc, t, scratch, ident, w_in, w_out, wsT, w_q)
        peer(nc, t, scratch, ident, w_q, spare, keysT)


def condition(nc, t, scratch, ident, w_in, w_out, wsT, keysT):
    ROWS = NS + 1
    CHUNKS = 6 * D // HALF
    RING = 3
    QUADS = 4
    Q = P // QUADS
    PER = D // HALF
    with ExitStack() as ctx:
        def sb(name, shape, dt=F32):
            return ctx.enter_context(nc.sbuf_tensor(name, shape, dt))

        def sem(name):
            return ctx.enter_context(nc.semaphore(name))

        c_rows = sb("c_rows", [P, D])
        c_act = sb("c_act", [P, D])
        key_rows = [c_rows, c_act]
        cT = sb("cT", [P, KD, Q])
        ada_w = [sb(f"ada_w{r}", [P, KD, HALF]) for r in range(RING)]
        ada_b = sb("ada_b", [P, CHUNKS, P])
        mod = sb("mod", [P, CHUNKS, P])
        gains = sb("gains", [P, 3, PER, P])
        w_s = sb("w_s", [P, G, P])
        x = sb("s_x", [P, PER, P])
        h = sb("s_h", [P, PER, P])
        hT = sb("s_hT", [P, KD, Q])
        y = sb("s_y", [P, PER, P])
        yT = hT
        x1 = sb("s_x1", [P, PER, P])
        h2, rest = h, y
        parts = w_s[:, :, :].rearrange("p g s -> p (g s)").bitcast(BF16)[:, 0:3 * D // QUADS].rearrange(
            "p (n a c) -> p n a c", n=3, a=PER)
        before = sb("s_before", [P, 2, P])
        conv_w = sb("s_conv_w", [P, P, 3])
        z = sb("s_z", [P, P])
        c_sb = sb("s_c", [P, P])
        v_dev = sb("s_v_dev", [P, P])
        v_gain = sb("s_v_gain", [P, P])
        w00 = sb("s_w00", [P, 1])
        b0 = sb("s_b0", [P, 1])
        gstat = sb("s_gstat", [P, 5])
        stat = sb("s_stat", [P, 3, 3])
        eps = sb("s_eps", [P, 1])
        zero = sb("s_zero", [P, P])
        same_row = sb("same_row", [P, QUADS, Q])
        ps_T = ctx.enter_context(nc.psum_tensor("ps_T", [P, HALF], F32))
        ps_wsT = ctx.enter_context(nc.psum_tensor("ps_wsT", [P, G, P], F32))
        ps_ada = [ctx.enter_context(nc.psum_tensor(f"ps_ada{r}", [P, P], F32)) for r in range(RING)]
        ps_p = ctx.enter_context(nc.psum_tensor("s_ps_p", [P, D], F32))
        ps_o = ctx.enter_context(nc.psum_tensor("s_ps_o", [P, PER, P], F32))
        ps_cT = ps_T[:, 0:KD * ROWS].rearrange("p (k r) -> p k r", r=ROWS)
        ps_sum = ps_T[:, HALF - 1:HALF]
        turned_rows = ps_T[:, 0:PER * P]
        ps_b, ps_c, ps_h, ps_u, ps_v = [ps_p[:, n * P:(n + 1) * P] for n in range(5)]

        def quad(ap, j):
            return ap.rearrange("r (n j c) -> r n j c", j=QUADS, c=P)[:, :, j, :]

        def sample_rows(ap, j):
            return ap[SEQ:SEQ + P, :].rearrange("(a i) (n j c) -> a i n j c", i=32, j=QUADS, c=P)[:, 0:2, :, j, :]

        c_landed = sem("c_landed")
        b_landed = sem("b_landed")
        gains_landed = sem("gains_landed")
        ws_landed = sem("ws_landed")
        keys_landed = sem("keys_landed")
        loaded = sem("s_loaded")
        win_landed = sem("win_landed")
        wout_landed = sem("wout_landed")
        ada_landed = [sem(f"ada_landed{r}") for r in range(RING)]
        silu_done = sem("silu_done")
        const_done = sem("const_done")
        cT_done = sem("cT_done")
        cT_copied = sem("cT_copied")
        ws_masked = sem("ws_masked")
        ws_turned = sem("ws_turned")
        ws_copied = sem("ws_copied")
        keys_turned = sem("keys_turned")
        keys_copied = sem("keys_copied")
        ada_done = [sem(f"ada_done{r}") for r in range(RING)]
        ada_added = [sem(f"ada_added{r}") for r in range(RING)]
        mod_step = sem("mod_step")
        mod_stored = sem("mod_stored")
        squared = sem("s_squared")
        ssq_total = sem("s_ssq_total")
        root_done = sem("s_root_done")
        var_root = sem("s_var_root")
        row_step = sem("s_row_step")
        turned = sem("s_turned")
        projected = sem("s_projected")
        summed = sem("s_summed")
        c_copied = sem("s_c_copied")
        part_done = sem("s_part_done")
        zero_stored = sem("s_zero_stored")
        stored = sem("s_stored")
        block = ctx.enter_context(nc.Block())

        SAMPLE_H, SAMPLE_HT, SAMPLE_Z, SAMPLE_VAR, SAMPLE_V, SAMPLE_Y, SAMPLE_YT, SAMPLE_X1, SAMPLE_H2 = (
            3, 4, 5, 15, 17, 20, 21, 24, 27)
        CONSTS = 6 + 2 + QUADS

        @block.sync
        def _(sp):
            sp.dma_start(c_rows[0:NS, :], t["c_sample"]).then_inc(c_landed, 16)
            sp.dma_start(c_rows[NS:ROWS, :], t["c_prompt"]).then_inc(c_landed, 16)
            with sp.Fori(0, CHUNKS // RING) as n:
                for r in range(RING):
                    sp.wait_ge(ada_done[r], 1 + n)
                    sp.dma_start(ada_w[r][:, :, :],
                                 t["w_ada"][0].rearrange("(k p) n -> p k n", p=P)[:, :, ds((n * RING + r) * HALF, HALF)]
                                 ).then_inc(ada_landed[r], 16)
            sp.dma_start(w_in[:, :, :], t["w_in"][0].rearrange("(k p) n -> p k n", p=P)).then_inc(win_landed, 16)
            sp.dma_start(w_out[:, :, :], t["w_out"][0].rearrange("(k p) n -> p k n", p=P)).then_inc(wout_landed, 16)
            sp.wait_ge(const_done, CONSTS)
            sp.dma_start(scratch["h2"][SEQ:SEQ + P, :].rearrange("p (a c) -> p a c", c=P),
                         zero[:, :].rearrange("p (a c) -> p a c", a=1).to_broadcast([P, KD, P])).then_inc(zero_stored, 16)
            for n in range(3):
                sp.dma_start(scratch["h2_parts"][n, SEQ:SEQ + P, :].rearrange("p (a c) -> p a c", c=2 * P),
                             zero[:, :].bitcast(BF16).rearrange("p (a c) -> p a c", a=1).to_broadcast([P, KD // 2, 2 * P])
                             ).then_inc(zero_stored, 16)
            sp.wait_ge(mod_step, 3)
            for j in range(QUADS):
                sp.dma_start(quad(scratch["mod"].rearrange("r f d -> r (f d)"), j), mod[Q * j:Q * j + ROWS, :, :]
                             ).then_inc(mod_stored, 16)
            for j in range(QUADS):
                if j == 0:
                    sp.wait_ge(row_step, SAMPLE_Z)
                sp.dma_start(t["new_conv_sample"][0, :, 0, j * P:(j + 1) * P], before[Q * j:Q * j + NS, 1, :]
                             ).then_inc(stored, 16)
                sp.dma_start(t["new_conv_sample"][0, :, 1, j * P:(j + 1) * P], z[Q * j:Q * j + NS, :]
                             ).then_inc(stored, 16)
            sp.wait_ge(row_step, SAMPLE_V)
            for j in range(QUADS):
                sp.dma_start(t["sgu_v_sample"][0, :, 0, j * P:(j + 1) * P], v_dev[Q * j:Q * j + NS, :]
                             ).then_inc(stored, 16)
            sp.wait_ge(row_step, SAMPLE_X1)
            for j in range(QUADS):
                sp.dma_start(sample_rows(scratch["x1"], j), x1[Q * j:Q * j + NS, :, :]).then_inc(stored, 16)
            sp.wait_ge(zero_stored, 64)
            sp.wait_ge(row_step, SAMPLE_H2)
            for j in range(QUADS):
                sp.dma_start(sample_rows(scratch["h2"], j), h2[Q * j:Q * j + NS, :, :]).then_inc(stored, 16)
            sp.wait_ge(part_done, 1)
            for j in range(QUADS):
                sp.dma_start(sample_rows(scratch["h2_parts"][0], j), parts[Q * j:Q * j + NS, 0, :, :]
                             ).then_inc(stored, 16)
            sp.wait_ge(stored, 16 * QUADS * 8)
            sp.wait_ge(mod_stored, 16 * QUADS)

        @block.scalar
        def _(act):
            for j in range(QUADS):
                act.dma_start(ada_b[Q * j:Q * j + Q, :, :], quad(t["b_ada"][0:1, :], j).to_broadcast([Q, CHUNKS, P])
                              ).then_inc(b_landed, 16)
            act.wait_ge(c_landed, 32)
            nc.scalar.activation(c_act[0:ROWS, :], c_rows[0:ROWS, :], ACT.Silu).then_inc(silu_done, 1)
            for j in range(QUADS):
                for n, name in enumerate(("g_pre_mix", "g_post_mix", "g_pre_ffn")):
                    act.dma_start(gains[Q * j:Q * j + Q, n, :, :], quad(t[name][0:1, :], j).to_broadcast([Q, PER, P])
                                  ).then_inc(gains_landed, 16)
            act.wait_ge(const_done, CONSTS)
            for j in range(QUADS):
                all_rows, rows, cols = slice(Q * j, Q * j + Q), slice(Q * j, Q * j + NS), slice(j * P, (j + 1) * P)
                act.dma_start(x[rows, :, :], quad(t["x_sample"].rearrange("b l d -> (b l) d"), j)).then_inc(loaded, 16)
                act.dma_start(before[rows, :, :], t["state_conv"][0][:, :, cols]).then_inc(loaded, 16)
                act.dma_start(conv_w[all_rows, :, :].rearrange("p c k -> p (c k)"),
                              t["conv_w"][0:1, cols, :].rearrange("a c k -> a (c k)").to_broadcast([Q, 3 * P])
                              ).then_inc(loaded, 16)
                act.dma_start(v_gain[all_rows, :], t["sgu_norm_g"][0:1, cols].to_broadcast([Q, P])).then_inc(loaded, 16)
                act.dma_start(w00[all_rows, :], t["w_s"][0:1, j, 0, 0:1].to_broadcast([Q, 1])).then_inc(loaded, 16)
                act.dma_start(b0[all_rows, :], t["b_s"][0:1, j, 0:1].to_broadcast([Q, 1])).then_inc(loaded, 16)
            act.dma_start(w_s[:, :, :], t["w_s"][0].rearrange("g t s -> t g s")).then_inc(ws_landed, 16)
            act.wait_ge(cT_done, 1)
            for i in range(2):
                act.dma_start(key_rows[i][:, :].rearrange("k (a c) -> k a c", c=P),
                              t["sub_keys"][0].rearrange("h p k c -> k (h p) c")[:, HEADS * i:HEADS * (i + 1), :]
                              ).then_inc(keys_landed, 16)

            def root(src, junk, acc):
                nc.scalar.activation(junk[:, :, :], src, ACT.Square, accum_out=stat[:, acc, 0:1]).then_inc(squared, 1)
                act.wait_ge(ssq_total, acc + 1)
                nc.scalar.activation(stat[:, acc, 1:2], ps_sum, ACT.Sqrt, scale=1.0 / D, bias=eps[:, 0:1]
                                     ).then_inc(root_done, 1)

            act.wait_ge(loaded, 16 * 6 * QUADS)
            root(x[:, :, :], x1, 0)
            act.wait_ge(projected, 1)
            nc.scalar.activation(c_sb[:, :], ps_c, ACT.Copy).then_inc(c_copied, 1)
            act.wait_ge(row_step, SAMPLE_VAR)
            nc.scalar.activation(gstat[:, 3:4], gstat[:, 2:3], ACT.Sqrt, scale=1.0 / P, bias=eps[:, 0:1]
                                 ).then_inc(var_root, 1)
            act.wait_ge(summed, 1)
            root(ps_o[:, :, :], x1, 1)
            act.wait_ge(row_step, SAMPLE_X1)
            root(x1[:, :, :], h2, 2)
            act.wait_ge(row_step, SAMPLE_H2)
            for n in range(3):
                if n:
                    act.wait_ge(row_step, SAMPLE_H2 + n)
                nc.scalar.activation(parts[:, n, :, :], (rest if n else h2)[:, :, :], ACT.Copy).then_inc(part_done, 1)
            act.wait_ge(part_done, 3)
            act.wait_ge(zero_stored, 64)
            for n in (1, 2):
                for j in range(QUADS):
                    act.dma_start(sample_rows(scratch["h2_parts"][n], j), parts[Q * j:Q * j + NS, n, :, :]
                                  ).then_inc(stored, 16)
            act.wait_ge(win_landed, 16)
            act.wait_ge(stored, 16 * QUADS * 8)

        @block.gpsimd
        def _(pool):
            pool.memset(ident[:, :], 0.0).then_inc(const_done, 1)
            pool.memset(cT[:, :, :], 0.0).then_inc(const_done, 1)
            pool.memset(x[:, :, :], 0.0).then_inc(const_done, 1)
            pool.memset(before[:, :, :], 0.0).then_inc(const_done, 1)
            pool.memset(eps[:, :], EPS).then_inc(const_done, 1)
            pool.memset(zero[:, :], 0.0).then_inc(const_done, 1)
            pool.wait_ge(const_done, 1)
            pool.affine_select(out=ident[:, :], in_=ident[:, :], compare_op=ALU.not_equal, fill=1.0, base=0,
                               pattern=[[-1, P]], channel_multiplier=1).then_inc(const_done, 1)
            pool.memset(same_row[:, :, :], 0.0).then_inc(const_done, 1)
            for j in range(QUADS):
                pool.wait_ge(const_done, 8 + j)
                pool.affine_select(out=same_row[:, :, :], in_=same_row[:, :, :], compare_op=ALU.not_equal, fill=1.0,
                                   base=-Q * j, pattern=[[0, QUADS], [-1, Q]], channel_multiplier=1
                                   ).then_inc(const_done, 1)
            pool.wait_ge(ws_landed, 16)
            pool.affine_select(out=w_s[:, :, :], in_=w_s[:, :, :], compare_op=ALU.is_ge, fill=0.0, base=0,
                               pattern=[[0, G], [-1, P]], channel_multiplier=1).then_inc(ws_masked, 1)

        @block.tensor
        def _(pe):
            for primed in ada_done:
                pe.sem_inc(primed, 1)
            pe.wait_ge(const_done, CONSTS)
            pe.wait_ge(silu_done, 1)
            for k in range(KD):
                last = pe.transpose(ps_cT[:, k, :], c_act[0:ROWS, k * P:(k + 1) * P], ident[0:ROWS, 0:ROWS])
            last.then_inc(cT_done, 1)
            pe.wait_ge(cT_copied, 1)
            with pe.Fori(0, CHUNKS // RING) as n:
                for r in range(RING):
                    pe.wait_ge(ada_landed[r], 16 * n + 16)
                    pe.wait_ge(ada_added[r], 1 + n)
                    for k in range(KD):
                        for j in range(QUADS):
                            last = pe.matmul(ps_ada[r][Q * j:Q * j + Q, :], cT[:, k, :],
                                             ada_w[r][:, k, j * P:(j + 1) * P], start=(k == 0), stop=(k == KD - 1))
                    last.then_inc(ada_done[r], 1)

            def total(acc):
                pe.wait_ge(squared, acc + 1)
                pe.matmul(ps_sum, same_row[:, :, :].rearrange("p a i -> p (a i)"), stat[:, acc, 0:1],
                          start=True, stop=True).then_inc(ssq_total, 1)

            def turn(rows):
                for n in range(PER):
                    last = pe.transpose(turned_rows[:, n * P:(n + 1) * P], rows[:, n, :], ident[:, :])
                last.then_inc(turned, 1)

            total(0)
            pe.wait_ge(ws_masked, 1)
            for g in range(G):
                last = pe.transpose(ps_wsT[:, g, :], w_s[:, g, :], ident[:, :])
            last.then_inc(ws_turned, 1)
            pe.wait_ge(keys_landed, 32)
            for r in range(4):
                if r >= 2:
                    pe.wait_ge(keys_copied, r - 1)
                for a in range(4):
                    c, at = 4 * (r % 2) + a, (r % 2) * HALF + a * P
                    last = pe.transpose(ps_p[:, at:at + P], key_rows[r // 2][:, c * P:(c + 1) * P], ident[:, :])
                last.then_inc(keys_turned, 1)
            pe.wait_ge(root_done, 1)
            pe.wait_ge(row_step, SAMPLE_H)
            turn(h)
            pe.wait_ge(row_step, SAMPLE_HT)
            pe.wait_ge(keys_copied, 4)
            pe.wait_ge(win_landed, 16)
            for k in range(KD):
                for j in range(QUADS):
                    cols = w_in[:, k, :].rearrange("p (n j c) -> p n j c", j=QUADS, c=P)[:, :, j, :]
                    pe.matmul(ps_p[Q * j:Q * j + Q, 0:4 * P], hT[:, k, :], cols[:, 0:4, :],
                              start=(k == 0), stop=(k == KD - 1))
                    last = pe.matmul(ps_v[Q * j:Q * j + Q, :], hT[:, k, :], cols[:, 4, :],
                                     start=(k == 0), stop=(k == KD - 1))
            last.then_inc(projected, 1)
            pe.wait_ge(row_step, SAMPLE_Y)
            turn(y)
            pe.wait_ge(row_step, SAMPLE_YT)
            pe.wait_ge(wout_landed, 16)
            for k in range(KD):
                for j in range(QUADS):
                    cols = w_out[:, k, :].rearrange("p (n j c) -> p n j c", j=QUADS, c=P)[:, :, j, :]
                    last = pe.matmul(ps_o[Q * j:Q * j + Q, :, :], yT[:, k, :], cols, start=(k == 0), stop=(k == KD - 1))
            last.then_inc(summed, 1)
            total(1)
            pe.wait_ge(root_done, 2)
            total(2)

        @block.vector
        def _(dve):
            for primed in ada_added:
                dve.sem_inc(primed, 1)
            dve.wait_ge(const_done, CONSTS)
            dve.wait_ge(cT_done, 1)
            dve.tensor_copy(cT[:, :, 0:ROWS], ps_cT).then_inc(cT_copied, 1)
            dve.wait_ge(b_landed, 16 * QUADS)
            with dve.Fori(0, CHUNKS // RING) as n:
                for r in range(RING):
                    dve.wait_ge(ada_done[r], 1 + n + 1)
                    chunk = ds(n * RING + r, 1)
                    dve.tensor_tensor(mod[:, chunk, :].rearrange("p a c -> p (a c)"), ps_ada[r][:, :],
                                      ada_b[:, chunk, :].rearrange("p a c -> p (a c)"), ALU.add
                                      ).then_inc(ada_added[r], 1)
            dve.wait_ge(gains_landed, 48 * QUADS)
            for r in range(RING):
                dve.wait_ge(ada_added[r], 1 + CHUNKS // RING)

            def row(n):
                return mod[:, PER * n:PER * n + PER, :]

            for dst, g in ((SCALE1, 0), (SCALE2, 2)):
                dve.scalar_tensor_tensor(out=row(dst), in0=row(dst), scalar=1.0, in1=gains[:, g, :, :],
                                         op0=ALU.add, op1=ALU.mult).then_inc(mod_step, 1)
            dve.tensor_tensor(row(GATE1), row(GATE1), gains[:, 1, :, :], ALU.mult).then_inc(mod_step, 1)
            dve.wait_ge(mod_step, 3)

            own = Steps(dve, row_step)

            def do(ins):
                own.did(ins)
                own.settle()

            dve.wait_ge(loaded, 16 * 6 * QUADS)
            dve.wait_ge(root_done, 1)
            do(dve.reciprocal(stat[:, 0, 2:3], stat[:, 0, 1:2]))
            do(dve.scalar_tensor_tensor(out=h[:, :, :], in0=x[:, :, :], scalar=stat[:, 0, 2:3], in1=row(SCALE1),
                                        op0=ALU.mult, op1=ALU.mult))
            do(dve.tensor_tensor(h[:, :, :], h[:, :, :], row(SHIFT1), ALU.add))
            assert own.n == SAMPLE_H
            dve.wait_ge(ws_turned, 1)
            dve.tensor_copy(wsT[:, :, :], ps_wsT[:, :, :]).then_inc(ws_copied, 1)
            for r in range(4):
                dve.wait_ge(keys_turned, r + 1)
                dve.tensor_copy(keysT[:, 4 * r:4 * r + 4, :].rearrange("p a k -> p (a k)"),
                                ps_p[:, (r % 2) * HALF:(r % 2 + 1) * HALF]).then_inc(keys_copied, 1)
            dve.wait_ge(turned, 1)
            do(dve.tensor_copy(hT[:, :, :].rearrange("p k r -> p (k r)"), turned_rows))
            assert own.n == SAMPLE_HT
            dve.wait_ge(projected, 1)
            dve.wait_ge(c_copied, 1)
            do(dve.tensor_tensor(z[:, :], c_sb[:, :], ps_h, ALU.mult))
            assert own.n == SAMPLE_Z
            do(dve.tensor_tensor(y[:, 0, :], before[:, 0, :], conv_w[:, :, 0], ALU.mult))
            do(dve.tensor_tensor(c_sb[:, :], before[:, 1, :], conv_w[:, :, 1], ALU.mult))
            do(dve.tensor_tensor(y[:, 0, :], y[:, 0, :], c_sb[:, :], ALU.add))
            do(dve.tensor_tensor(c_sb[:, :], z[:, :], conv_w[:, :, 2], ALU.mult))
            do(dve.tensor_tensor(y[:, 0, :], y[:, 0, :], c_sb[:, :], ALU.add))
            do(dve.tensor_reduce(gstat[:, 0:1], ps_v, AX, ALU.add))
            do(dve.tensor_scalar(gstat[:, 1:2], gstat[:, 0:1], -1.0 / P, None, ALU.mult))
            do(dve.tensor_scalar(v_dev[:, :], ps_v, gstat[:, 1:2], None, ALU.add))
            do(dve.tensor_tensor(c_sb[:, :], v_dev[:, :], v_dev[:, :], ALU.mult))
            do(dve.tensor_reduce(gstat[:, 2:3], c_sb[:, :], AX, ALU.add))
            assert own.n == SAMPLE_VAR
            dve.wait_ge(var_root, 1)
            do(dve.reciprocal(gstat[:, 4:5], gstat[:, 3:4]))
            do(dve.scalar_tensor_tensor(out=v_dev[:, :], in0=v_dev[:, :], scalar=gstat[:, 4:5], in1=v_gain[:, :],
                                        op0=ALU.mult, op1=ALU.mult))
            assert own.n == SAMPLE_V
            do(dve.tensor_scalar(c_sb[:, :], v_dev[:, :], w00[:, 0:1], b0[:, 0:1], ALU.mult, ALU.add))
            do(dve.tensor_tensor(y[:, 1, :], c_sb[:, :], ps_u, ALU.mult))
            do(dve.tensor_tensor(y[:, 0, :], y[:, 0, :], ps_b, ALU.mult))
            assert own.n == SAMPLE_Y
            dve.wait_ge(turned, 2)
            do(dve.tensor_copy(yT[:, :, :].rearrange("p k r -> p (k r)"), turned_rows))
            assert own.n == SAMPLE_YT
            dve.wait_ge(root_done, 2)
            do(dve.reciprocal(stat[:, 1, 2:3], stat[:, 1, 1:2]))
            do(dve.scalar_tensor_tensor(out=x1[:, :, :], in0=ps_o[:, :, :], scalar=stat[:, 1, 2:3], in1=row(GATE1),
                                        op0=ALU.mult, op1=ALU.mult))
            do(dve.tensor_tensor(x1[:, :, :], x1[:, :, :], x[:, :, :], ALU.add))
            assert own.n == SAMPLE_X1
            dve.wait_ge(root_done, 3)
            do(dve.reciprocal(stat[:, 2, 2:3], stat[:, 2, 1:2]))
            do(dve.scalar_tensor_tensor(out=h2[:, :, :], in0=x1[:, :, :], scalar=stat[:, 2, 2:3], in1=row(SCALE2),
                                        op0=ALU.mult, op1=ALU.mult))
            do(dve.tensor_tensor(h2[:, :, :], h2[:, :, :], row(SHIFT2), ALU.add))
            assert own.n == SAMPLE_H2
            for n in range(2):
                dve.wait_ge(part_done, n + 1)
                do(dve.tensor_tensor(rest[:, :, :], (rest if n else h2)[:, :, :], parts[:, n, :, :], ALU.subtract))


def mix_prompt(nc, t, scratch, ident, w_in, w_out, wsT, w_q):
    with ExitStack() as ctx:
        def sb(name, shape, dt=F32):
            return ctx.enter_context(nc.sbuf_tensor(name, shape, dt))

        def sem(name):
            return ctx.enter_context(nc.semaphore(name))

        hT = sb("hT", [P, KD, HALF])
        yT = sb("yT", [P, KD, HALF])
        z = sb("z", [P, CB, 2 + HALF])
        x_in = [sb(f"x_in{i}", [P, D]) for i in range(2)]
        rows = [sb(f"rows{i}", [P, D]) for i in range(2)]
        x1w, h2w = rows
        gate1_b = sb("gate1_b", [P, D])
        scale2_b = sb("scale2_b", [P, D])
        shift2_b = sb("shift2_b", [P, D])
        scale1_f = sb("scale1_f", [P, KD])
        shift1_f = sb("shift1_f", [P, KD])
        conv_w = sb("conv_w_f", [P, CB, 3])
        rest = sb("rest", [P, 2 * CONV])
        v_dev, v_sq = rest[:, 0:CONV], rest[:, CONV:2 * CONV]
        v_norm = sb("v_norm", [P, CONV])
        v_gain = sb("v_gain", [P, CONV])
        c_sb, y_sb = v_dev, v_sq
        bs_row = sb("bs_row", [1, CONV])
        ones_row = sb("ones_row", [1, P])
        eps = sb("eps", [P, 1])
        junk = v_norm[:, :].bitcast(BF16)
        parts = sb("parts", [P, 3, D], BF16)
        stat = sb("stat", [P, 3, 3])
        gstat = sb("gstat", [P, 5, G])
        banks = [ctx.enter_context(nc.psum_tensor(f"mix_bank{i}", [P, HALF], F32)) for i in range(2)]
        pair = [ctx.enter_context(nc.psum_tensor(f"mix_pair{i}", [P, D], F32)) for i in range(3)]
        ps_xT = [banks, [pair[1][:, 0:HALF], pair[1][:, HALF:D]]]
        ps_mixed = banks[1]
        ps_c, ps_h = pair[2][:, 0:HALF], pair[2][:, HALF:D]
        ps_v = [ps_h, banks[0]]
        ps_b = pair[0][:, 0:HALF]
        ps_u = [pair[1][:, 0:HALF], pair[1][:, HALF:D]]
        ps_o = [pair[0], pair[2]]

        wq_landed = sem("wq_landed")
        mods_landed = sem("mods_landed")
        x_landed = [sem(f"x_landed{i}") for i in range(2)]
        xr_landed = [sem(f"xr_landed{i}") for i in range(2)]
        const_done = sem("mconst_done")
        ssq_done = sem("ssq_done")
        dve_x = sem("dve_x")
        xn_done = sem("xn_done")
        xT_done = sem("xT_done")
        hT_done = sem("hT_done")
        v_done = sem("v_done")
        dve_v = sem("dve_v")
        var_ready = sem("var_ready")
        vstd_done = sem("vstd_done")
        vn_done = sem("vn_done")
        mixed_done = sem("mixed_done")
        mixed_kept = sem("mixed_kept")
        c_done = sem("c_done")
        h_done = sem("h_done")
        b_done = sem("b_done")
        c_copied = sem("c_copied")
        dve_conv = sem("dve_conv")
        conv_done = sem("conv_done")
        u_done = sem("u_done")
        gated_done = sem("gated_done")
        tail_moved = sem("tail_moved")
        o_done = sem("o_done")
        ossq_done = sem("ossq_done")
        dve_o = sem("dve_o")
        o_used = sem("o_used")
        x1_done = sem("x1_done")
        x1ssq_done = sem("x1ssq_done")
        h2_done = sem("h2_done")
        part_done = [sem(f"part_done{i}") for i in range(3)]
        rest_scaled = sem("rest_scaled")
        rest_done = [sem(f"rest_done{i}") for i in range(2)]
        x1_stored = sem("x1_stored")
        h2_stored = sem("h2_stored")
        parts_stored = sem("parts_stored")
        state_stored = sem("state_stored")
        x1_left, h2_left, parts_left = sem("x1_left"), sem("h2_left"), sem("parts_left")
        act_own = sem("act_own")
        sp_noted = sem("mix_sp_noted")
        block = ctx.enter_context(nc.Block())

        x_rows = t["x_prompt"][0]
        PASSES = SEQ // HALF

        def store(sp, h, b):
            row = h * HALF + b * P
            sp.wait_ge(x1_done, 1 + 4 * h + b + 1)
            sp.dma_start(scratch["x1"][ds(row, P), :], x1w[:, :]).then_inc(x1_stored, 16)
            sp.wait_ge(h2_done, 4 * h + b + 1)
            sp.dma_start(scratch["h2"][ds(row, P), :], h2w[:, :]).then_inc(h2_stored, 16)
            for n in range(3):
                wait_apart(sp, sp_noted, (part_done[n], 1 + 4 * h + b + 1))
                sp.dma_start(scratch["h2_parts"][n, ds(row, P), :], parts[:, n, :]).then_inc(parts_stored, 16)
            sp.wait_ge(x1_stored, 64 * h + 16 * b + 16)
            sp.sem_inc(x1_left, 1)
            sp.wait_ge(h2_stored, 64 * h + 16 * b + 16)
            sp.sem_inc(h2_left, 1)
            sp.wait_ge(parts_stored, 192 * h + 48 * b + 48)
            sp.sem_inc(parts_left, 1)

        def load_x(sp, h, b, landed):
            sp.dma_start(x_in[b % 2][:, :], x_rows[h * HALF + b * P:h * HALF + (b + 1) * P, :]).then_inc(landed[b % 2], 16)

        @block.sync
        def _(sp):
            load_x(sp, 0, 0, x_landed)
            load_x(sp, 0, 1, x_landed)
            mod = scratch["mod"]
            with nc.allow_non_contiguous_dma("feature-major vectors"):
                sp.dma_start(scale1_f[:, :], mod[NS, SCALE1, :].rearrange("(k p) -> p k", p=P)).then_inc(mods_landed, 16)
                sp.dma_start(shift1_f[:, :], mod[NS, SHIFT1, :].rearrange("(k p) -> p k", p=P)).then_inc(mods_landed, 16)
                sp.dma_start(conv_w[:, :, :], t["conv_w"][0].rearrange("(c p) k -> p c k", p=P)).then_inc(mods_landed, 16)
            for dst, n in ((gate1_b, GATE1), (scale2_b, SCALE2), (shift2_b, SHIFT2)):
                sp.dma_start(dst[:, :], mod[NS:NS + 1, n, :].to_broadcast([P, D])).then_inc(mods_landed, 16)
            sp.dma_start(v_gain[:, :], t["sgu_norm_g"][0:1, :].to_broadcast([P, CONV])).then_inc(mods_landed, 16)
            sp.dma_start(bs_row[:, :], t["b_s"].rearrange("a g t -> a (g t)")).then_inc(mods_landed, 16)

            for primed in (x1_left, h2_left, parts_left):
                sp.sem_inc(primed, 1)
            for h in range(PASSES):
                for b in range(TB):
                    if 4 * h + b >= 2:
                        sp.wait_ge(xn_done, 1 + 4 * h + b - 1)
                        load_x(sp, h, b, x_landed)
            for h in range(PASSES):
                for b in range(TB):
                    if 4 * h + b < 2:
                        sp.wait_ge(xn_done, 1 + 4 * PASSES)
                    else:
                        sp.wait_ge(x1_done, 1 + 4 * h + b - 1)
                    load_x(sp, h, b, xr_landed)
                    if b >= 1:
                        store(sp, h, b - 1)
                    if h == PASSES - 1 and b == 2:
                        sp.wait_ge(tail_moved, 1 + PASSES)
                        with nc.allow_non_contiguous_dma("conv state, feature-major"):
                            for c in range(CB):
                                sp.dma_start(t["new_conv_prompt"][0, 0, :, c * P:(c + 1) * P].rearrange("k p -> p k"),
                                             z[:, c, 0:2]).then_inc(state_stored, 16)
                store(sp, h, TB - 1)
            sp.wait_ge(state_stored, 16 * CB)
            sp.wait_ge(x1_stored, 16 * 8)
            sp.wait_ge(h2_stored, 16 * 8)
            sp.wait_ge(parts_stored, 48 * 8)

        @block.gpsimd
        def _(pool):
            pool.memset(ones_row[:, :], 1.0).then_inc(const_done, 1)
            pool.memset(eps[:, :], EPS).then_inc(const_done, 1)
            pool.memset(z[:, :, 0:2], 0.0).then_inc(const_done, 1)
            pool.wait_ge(u_done, 2 * G)
            pool.dma_start(w_q[:, :, :], t["w_q"][0].rearrange("(k p) n -> p k n", p=P)).then_inc(wq_landed, 16)
            pool.wait_ge(wq_landed, 16)

        @block.scalar
        def _(act):
            for primed in (mixed_kept, *part_done):
                act.sem_inc(primed, 1)
            act.wait_ge(const_done, 3)

            def std(src, width, done, base, acc):
                nc.scalar.activation(junk[:, 0:width], src, ACT.Square, accum_out=stat[:, acc, 0:1]).then_inc(act_own, 1)
                act.wait_ge(act_own, base)
                nc.scalar.activation(stat[:, acc, 1:2], stat[:, acc, 0:1], ACT.Sqrt, scale=1.0 / D,
                                     bias=eps[:, 0:1]).then_inc(done, 1)

            def norms(h):
                for b in range(TB + 1):
                    if b < TB:
                        act.wait_ge(x_landed[b % 2], 32 * h + 16 * (b // 2) + 16)
                        act.wait_ge(dve_x, 1 + 4 * h + b)
                        std(x_in[b % 2][:, :], D, ssq_done, 4 * h + b + 1, 0)
                    if b >= 1:
                        c = b - 1
                        act.wait_ge(mods_landed, 16 * 8)
                        act.wait_ge(xT_done, 4 * h + c + 1)
                        for k in range(KD):
                            last = nc.scalar.activation(hT[:, k, c * P:(c + 1) * P],
                                                        ps_xT[c % 2][k // 4][:, k % 4 * P:(k % 4 + 1) * P],
                                                        ACT.Identity, scale=scale1_f[:, k:k + 1],
                                                        bias=shift1_f[:, k:k + 1])
                        last.then_inc(hT_done, 1)

            norms(0)
            for h in range(PASSES):
                for b in range(TB + 1):
                    if b < TB:
                        act.wait_ge(var_ready, 4 * h + b + 1)
                        nc.scalar.activation(gstat[:, 3, :], gstat[:, 2, :], ACT.Sqrt, scale=1.0 / P,
                                             bias=eps[:, 0:1]).then_inc(vstd_done, 1)
                    if b >= 1:
                        c = b - 1
                        act.wait_ge(mixed_done, 1 + 4 * h + c + 1)
                        nc.scalar.activation(yT[:, CB:KD, c * P:(c + 1) * P],
                                             ps_mixed[:, :].rearrange("p (g n) -> p g n", g=G), ACT.Copy
                                             ).then_inc(mixed_kept, 1)
                for c in range(CB):
                    act.wait_ge(c_done, 4 * h + c + 1)
                    if c >= 1:
                        act.wait_ge(dve_conv, 16 * h + 4 * (c - 1) + 1)
                    else:
                        act.wait_ge(vn_done, 1 + 4 * h + 4)
                    nc.scalar.activation(c_sb[:, :], ps_c, ACT.Copy).then_inc(c_copied, 1)
                if h + 1 < PASSES:
                    norms(h + 1)
                for b in range(TB):
                    act.wait_ge(o_done, 4 * h + b + 1)
                    act.wait_ge(dve_o, 1 + 8 * h + 2 * b)
                    std(ps_o[b % 2][:, :], D, ossq_done, 4 * PASSES + 8 * h + 2 * b + 1, 1)
                    act.wait_ge(x1_done, 1 + 4 * h + b + 1)
                    std(x1w[:, :], D, x1ssq_done, 4 * PASSES + 8 * h + 2 * b + 2, 2)
                    act.wait_ge(h2_done, 4 * h + b + 1)
                    act.wait_ge(parts_left, 1 + 4 * h + b)
                    nc.scalar.activation(parts[:, 0, :], h2w[:, :], ACT.Copy).then_inc(part_done[0], 1)
                    for n in range(2):
                        act.wait_ge(rest_done[n], 4 * h + b + 1)
                        nc.scalar.activation(parts[:, n + 1, :], rest[:, :], ACT.Copy).then_inc(part_done[n + 1], 1)

        @block.vector
        def _(dve):
            for primed in (x1_done, dve_x, dve_o, xn_done, tail_moved, o_used, vn_done):
                dve.sem_inc(primed, 1)
            dve.wait_ge(const_done, 3)

            def groups(ap):
                return ap.rearrange("p (g n) -> p g n", g=G)

            def per_group(n):
                return gstat[:, n, :].rearrange("p (g o) -> p g o", o=1).to_broadcast([P, G, P])

            def norm(h, b):
                dve.wait_ge(ssq_done, 4 * h + b + 1)
                if 4 * h + b >= 2:
                    dve.wait_ge(xT_done, 4 * h + b - 1)
                dve.wait_ge(xn_done, 1 + 4 * h + b)
                dve.reciprocal(stat[:, 0, 2:3], stat[:, 0, 1:2]).then_inc(dve_x, 1)
                dve.wait_ge(dve_x, 1 + 4 * h + b + 1)
                dve.tensor_scalar(rows[b % 2][:, :], x_in[b % 2][:, :], stat[:, 0, 2:3], None, ALU.mult
                                  ).then_inc(xn_done, 1)

            for b in range(TB):
                norm(0, b)
            dve.wait_ge(mods_landed, 16 * 8)
            for h in range(PASSES):
                if h:
                    dve.wait_ge(part_done[2], 1 + 4 * h)
                for b in range(TB):
                    dve.wait_ge(v_done, 4 * h + b + 1)
                    own = Steps(dve, dve_v, 24 * h + 6 * b)
                    own.did(dve.tensor_reduce(gstat[:, 0, :], groups(ps_v[b % 2]), AX, ALU.add))
                    own.settle()
                    own.did(dve.tensor_scalar(gstat[:, 1, :], gstat[:, 0, :], -1.0 / P, None, ALU.mult))
                    own.settle()
                    own.did(dve.tensor_tensor(groups(v_dev[:, :]), groups(ps_v[b % 2]), per_group(1), ALU.add))
                    own.settle()
                    own.did(dve.tensor_tensor(v_sq[:, :], v_dev[:, :], v_dev[:, :], ALU.mult))
                    own.settle()
                    dve.tensor_reduce(gstat[:, 2, :], groups(v_sq[:, :]), AX, ALU.add).then_inc(var_ready, 1)
                    dve.wait_ge(vstd_done, 4 * h + b + 1)
                    own.did(dve.reciprocal(gstat[:, 4, :], gstat[:, 3, :]))
                    own.settle()
                    own.did(dve.tensor_tensor(groups(v_dev[:, :]), groups(v_dev[:, :]), per_group(4), ALU.mult))
                    own.settle()
                    dve.wait_ge(mixed_done, 1 + 4 * h + b)
                    dve.tensor_tensor(v_norm[:, :], v_dev[:, :], v_gain[:, :], ALU.mult).then_inc(vn_done, 1)
                dve.wait_ge(tail_moved, 1 + h)
                for c in range(CB):
                    own = Steps(dve, dve_conv, 16 * h + 4 * c)
                    dve.wait_ge(c_copied, 4 * h + c + 1)
                    dve.wait_ge(h_done, 4 * h + c + 1)
                    own.did(dve.tensor_tensor(z[:, c, 2:2 + HALF], c_sb[:, :], ps_h, ALU.mult))
                    own.settle()
                    if c >= 1:
                        dve.wait_ge(conv_done, 4 * h + c)
                    own.did(dve.tensor_scalar(y_sb[:, :], z[:, c, 0:HALF], conv_w[:, c, 0:1], None, ALU.mult))
                    for k in (1, 2):
                        own.settle()
                        own.did(dve.scalar_tensor_tensor(out=y_sb[:, :], in0=z[:, c, k:k + HALF],
                                                         scalar=conv_w[:, c, k:k + 1], in1=y_sb[:, :],
                                                         op0=ALU.mult, op1=ALU.add))
                    own.settle()
                    dve.wait_ge(b_done, 4 * h + c + 1)
                    dve.tensor_tensor(yT[:, c, :], y_sb[:, :], ps_b, ALU.mult).then_inc(conv_done, 1)
                dve.tensor_copy(z[:, :, 0:2], z[:, :, HALF:HALF + 2]).then_inc(tail_moved, 1)
                if h + 1 < PASSES:
                    norm(h + 1, 0)
                    norm(h + 1, 1)
                for g in range(G):
                    dve.wait_ge(mixed_kept, 1 + 4 * h + 4)
                    dve.wait_ge(u_done, 4 * h + g + 1)
                    dve.tensor_tensor(yT[:, CB + g, :], yT[:, CB + g, :], ps_u[g % 2], ALU.mult
                                      ).then_inc(gated_done, 1)
                if h + 1 < PASSES:
                    norm(h + 1, 2)
                    norm(h + 1, 3)
                    dve.wait_ge(xT_done, 4 * (h + 1) + 4)
                for b in range(TB):
                    own = Steps(dve, dve_o, 1 + 8 * h + 2 * b)
                    dve.wait_ge(ossq_done, 4 * h + b + 1)
                    own.did(dve.reciprocal(stat[:, 1, 2:3], stat[:, 1, 1:2]))
                    own.settle()
                    dve.wait_ge(x1_left, 1 + 4 * h + b)
                    dve.scalar_tensor_tensor(out=x1w[:, :], in0=ps_o[b % 2][:, :], scalar=stat[:, 1, 2:3],
                                             in1=gate1_b[:, :], op0=ALU.mult, op1=ALU.mult).then_inc(o_used, 1)
                    dve.wait_ge(o_used, 1 + 4 * h + b + 1)
                    dve.wait_ge(xr_landed[b % 2], 32 * h + 16 * (b // 2) + 16)
                    dve.tensor_tensor(x1w[:, :], x1w[:, :], x_in[b % 2][:, :], ALU.add).then_inc(x1_done, 1)
                    dve.wait_ge(x1ssq_done, 4 * h + b + 1)
                    own.did(dve.reciprocal(stat[:, 2, 2:3], stat[:, 2, 1:2]))
                    own.settle()
                    dve.wait_ge(h2_left, 1 + 4 * h + b)
                    dve.wait_ge(part_done[2], 1 + 4 * h + b)
                    dve.scalar_tensor_tensor(out=rest[:, :], in0=x1w[:, :], scalar=stat[:, 2, 2:3],
                                             in1=scale2_b[:, :], op0=ALU.mult, op1=ALU.mult).then_inc(rest_scaled, 1)
                    dve.wait_ge(rest_scaled, 4 * h + b + 1)
                    dve.tensor_tensor(h2w[:, :], rest[:, :], shift2_b[:, :], ALU.add).then_inc(h2_done, 1)
                    for n, src in ((0, h2w), (1, rest)):
                        if n == 0:
                            dve.wait_ge(h2_done, 4 * h + b + 1)
                        dve.wait_ge(part_done[n], 1 + 4 * h + b + 1)
                        dve.tensor_tensor(rest[:, :], src[:, :], parts[:, n, :], ALU.subtract
                                          ).then_inc(rest_done[n], 1)

        @block.tensor
        def _(pe):
            pe.sem_inc(mixed_done, 1)

            def project(out, col):
                for k in range(KD):
                    last = pe.matmul(out, w_in[:, k, col:col + P], hT[:, k, :], start=(k == 0), stop=(k == KD - 1))
                return last

            def turn(h, b):
                pe.wait_ge(xn_done, 1 + 4 * h + b + 1)
                if h and b == 0:
                    pe.wait_ge(gated_done, 4 * h)
                    pe.wait_ge(mixed_kept, 1 + 4 * h)
                if b >= 2:
                    pe.wait_ge(hT_done, 4 * h + b - 1)
                for k in range(KD):
                    last = pe.transpose(ps_xT[b % 2][k // 4][:, k % 4 * P:(k % 4 + 1) * P],
                                        rows[b % 2][:, k * P:(k + 1) * P], ident[:, :])
                last.then_inc(xT_done, 1)

            def mixed(h, b):
                pe.wait_ge(vn_done, 1 + 4 * h + b + 1)
                pe.wait_ge(mixed_kept, 1 + 4 * h + b)
                for g in range(G):
                    pe.matmul(ps_mixed[:, g * P:(g + 1) * P], v_norm[:, g * P:(g + 1) * P], wsT[:, g, :],
                              start=True, stop=False)
                    last = pe.matmul(ps_mixed[:, g * P:(g + 1) * P], ones_row[:, :],
                                     bs_row[:, g * P:(g + 1) * P], start=False, stop=True)
                last.then_inc(mixed_done, 1)

            for b in range(TB):
                turn(0, b)
            for h in range(PASSES):
                for b in range(TB):
                    if b == 0:
                        pe.wait_ge(o_used, 1 + 4 * h)
                        pe.wait_ge(hT_done, 4 * h + 1)
                    else:
                        pe.wait_ge(hT_done, 4 * h + max(b + 1, 3))
                    if b >= 2:
                        pe.wait_ge(vn_done, 1 + 4 * h + b - 1)
                    for k in range(KD):
                        last = pe.matmul(ps_v[b % 2][:, :], hT[:, k, b * P:(b + 1) * P],
                                         w_in[:, k, 3 * CONV + CONV:IN_DIM], start=(k == 0), stop=(k == KD - 1))
                    last.then_inc(v_done, 1)
                    if b >= 1:
                        mixed(h, b - 1)
                pe.wait_ge(hT_done, 4 * h + 4)
                for c in range(CB):
                    if c >= 1:
                        pe.wait_ge(c_copied, 4 * h + c)
                    project(ps_c, CONV + c * P).then_inc(c_done, 1)
                    if c == 0:
                        mixed(h, TB - 1)
                    if c >= 1:
                        pe.wait_ge(dve_conv, 16 * h + 4 * (c - 1) + 1)
                    project(ps_h, 2 * CONV + c * P).then_inc(h_done, 1)
                    if c >= 1:
                        pe.wait_ge(conv_done, 4 * h + c)
                    project(ps_b, c * P).then_inc(b_done, 1)
                for g in range(G):
                    if g >= 2:
                        pe.wait_ge(gated_done, 4 * h + g - 1)
                    project(ps_u[g % 2], 3 * CONV + g * P).then_inc(u_done, 1)
                pe.wait_ge(gated_done, 4 * h + 4)
                pe.wait_ge(conv_done, 4 * h + 4)
                if h + 1 < PASSES:
                    turn(h + 1, 0)
                    turn(h + 1, 1)
                for b in range(TB):
                    if b == 1 and h + 1 < PASSES:
                        turn(h + 1, 2)
                        turn(h + 1, 3)
                    if b >= 2:
                        pe.wait_ge(o_used, 1 + 4 * h + b - 1)
                    for n in range(2):
                        for k in range(KD):
                            last = pe.matmul(ps_o[b % 2][:, n * HALF:(n + 1) * HALF], yT[:, k, b * P:(b + 1) * P],
                                             w_out[:, k, n * HALF:(n + 1) * HALF], start=(k == 0), stop=(k == KD - 1))
                    last.then_inc(o_done, 1)


def peer(nc, t, scratch, ident, w_q, spare, keysT):
    RING = 8
    BODY = 8
    CAND = TOPK * TOPK
    CHAIN = 28
    SEARCHED = 6
    PAIRS = HEADS - 2
    with ExitStack() as ctx:
        def sb(name, shape, dt=F32):
            return ctx.enter_context(nc.sbuf_tensor(name, shape, dt))

        def sem(name):
            return ctx.enter_context(nc.semaphore(name))

        h2_in = sb("h2_in", [P, D])
        h2T = sb("h2T", [P, KD, P])
        h2_bf = sb("h2_bf", [96, 2, 4, D], BF16)
        u_rows = spare + [sb(f"u_rows{s}", [P, D]) for s in range(len(spare), RING)]
        v_rows = [sb(f"v_rows{s}", [P, D]) for s in range(RING)]
        q_sb = sb("q_sb", [P, QCOLS])
        qT_sb = sb("qT_sb", [P, QCOLS])
        s_sb = sb("s_sb", [P, 2, KEYS])
        s_less = sb("s_less", [P, 2, KEYS])
        top_v = sb("top_v", [P, 2, TOPK])
        top_i = sb("top_i", [P, 2, TOPK], U32)
        top_f = sb("top_f", [P, 2, TOPK])
        cand = sb("cand", [P, TOPK, TOPK])
        cand_less = sb("cand_less", [P, CAND])
        pair_v = sb("pair_v", [P, TOPK])
        pair_i = sb("pair_i", [P, TOPK], U32)
        pair_hl = sb("pair_hl", [P, 2, TOPK], U32)
        pair_f = sb("pair_f", [P, 2, TOPK])
        pick = sb("pick", [P, 2, TOPK, TOPK])
        pick_f = sb("pick_f", [P, 2, TOPK])
        count_i = sb("count_i", [P, TOPK], mybir.dt.int32)
        count = sb("count", [P, TOPK])
        expert_f = sb("expert_f", [P, HEADS * TOPK])
        best = sb("best", [P, HEADS, TOPK])
        gate = sb("gate", [P, HEADS, TOPK])
        total = sb("total", [P, HEADS])
        inverse = sb("inverse", [P, HEADS])
        expertT = sb("expertT", [P, NBLK, 4, 32], U32)
        gateT = sb("gateT", [P, NBLK, 4, 32])
        u_idx = [sb(f"u_idx{i}", [P, BODY], U32) for i in range(2)]
        v_idx = [sb(f"v_idx{i}", [P, BODY], U32) for i in range(2)]
        dot = [sb(f"dot{i}", [P, 4]) for i in range(2)]
        act_u = [sb(f"act_u{i}", [P, 4]) for i in range(2)]
        weight = [sb(f"weight{s}", [P, 32]) for s in range(BODY)]
        window = sb("window", [P, 63])
        pick_row = sb("pick_row", [96, 32], BF16)
        y_stat = sb("y_stat", [P, 3])
        eps = sb("p_eps", [P, 1])
        x1_in = sb("x1_in", [P, D])
        out_rows = sb("out_rows", [P, D])
        gate2_b = sb("gate2_b", [P, D])
        gate2_s = sb("gate2_s", [P, D])
        zeros = sb("zeros", [P, HALF], BF16)
        gain2 = v_rows[0]

        ps_x = [ctx.enter_context(nc.psum_tensor(f"ps_x{i}", [P, D], F32)) for i in range(2)]
        ps_y = ctx.enter_context(nc.psum_tensor("ps_y", [P, D], F32))
        ps_a = ctx.enter_context(nc.psum_tensor("ps_a", [P, 4, P], F32))
        ps_b = ctx.enter_context(nc.psum_tensor("ps_b2", [P, 4, P], F32))
        flat_a = ps_a[:, :, :].rearrange("p a b -> p (a b)")
        flat_b = ps_b[:, :, :].rearrange("p a b -> p (a b)")

        gains_landed = sem("p_gains_landed")
        h2_landed = sem("h2_landed")
        bf_landed = sem("bf_landed")
        x1_landed = sem("x1_landed")
        u_landed = [sem(f"u_landed{s}") for s in range(RING)]
        v_landed = [sem(f"v_landed{s}") for s in range(RING)]
        v_used = [sem(f"v_used{s}") for s in range(RING)]
        const_done = sem("p_const_done")
        sp_noted, act_noted = sem("sp_noted"), sem("act_noted")
        dve_noted, pool_noted = sem("dve_noted"), sem("pool_noted")
        gate2_done = sem("gate2_done")
        h2_turned = sem("h2_turned")
        h2T_done = sem("h2T_done")
        q_done = sem("q_done")
        q_copied = sem("q_copied")
        qT_done = sem("qT_done")
        qT_copied = sem("qT_copied")
        s_done = sem("s_done")
        s_copied = sem("s_copied")
        head_step = sem("head_step")
        soft_step = sem("soft_step")
        exp_done = sem("exp_done")
        picked_turned = sem("picked_turned")
        expert_ready = sem("expert_ready")
        gate_ready = sem("gate_ready")
        u_idx_ready = sem("u_idx_ready")
        v_idx_ready = sem("v_idx_ready")
        x_spread = sem("x_spread")
        dots_done = sem("dots_done")
        gelu_done = sem("gelu_done")
        weight_done = sem("weight_done")
        y_done = sem("y_done")
        y_ssq = sem("y_ssq")
        y_std = sem("y_std")
        y_inverse = sem("y_inverse")
        y_used = sem("y_used")
        out_done = sem("out_done")
        out_stored = sem("out_stored")
        out_left = sem("out_left")
        block = ctx.enter_context(nc.Block())

        def load_rows(sp, blk):
            wait_apart(sp, sp_noted, (h2_turned, 2 * blk))
            sp.dma_start(h2_in[:, :], scratch["h2"][ds(blk * P, P), :]).then_inc(h2_landed, 16)

        def load_parts(sp, blk):
            wait_apart(sp, sp_noted, (dots_done, 1 + P * (blk - 1)))
            for n in range(3):
                sp.dma_start(h2_bf[32 * n:32 * n + 32, ds(blk % 2, 1), :, :].rearrange("p a j d -> p (a j) d"),
                             scratch["h2_parts"][n, ds(blk * P, P), :].rearrange("(j i) d -> i j d", i=32)
                             ).then_inc(bf_landed, 16)

        @block.sync
        def _(sp):
            sp.sem_inc(out_left, 1)
            sp.dma_start(h2_in[:, :], scratch["h2"][0:P, :]).then_inc(h2_landed, 16)
            for n in range(3):
                sp.dma_start(h2_bf[32 * n:32 * n + 32, 0, :, :],
                             scratch["h2_parts"][n, 0:P, :].rearrange("(j i) d -> i j d", i=32)).then_inc(bf_landed, 16)
            load_rows(sp, 1)
            sp.wait_ge(dots_done, 1 + 1)
            load_parts(sp, 1)

            def rows_of(b, more):
                if more:
                    load_rows(sp, b + 2)
                sp.wait_ge(out_done, 1 + b)
                sp.dma_start(x1_in[:, :], scratch["x1"][ds(b * P, P), :]).then_inc(x1_landed, 16)
                if more:
                    load_parts(sp, b + 2)
                sp.wait_ge(out_done, 1 + b + 1)
                sp.dma_start(t["y_prompt"][0, ds(b * P, P), :], out_rows[:, :]).then_inc(out_stored, 16)
                sp.wait_ge(out_stored, 16 * b + 16)
                sp.sem_inc(out_left, 1)

            with sp.Fori(0, NBLK - 2) as b:
                rows_of(b, True)
            rows_of(NBLK - 2, False)
            for j in range(4):
                sp.dma_start(x1_in[32 * j:32 * j + 2, :], scratch["x1"][SEQ + 32 * j:SEQ + 32 * j + 2, :]
                             ).then_inc(x1_landed, 16)
            sp.wait_ge(out_done, 1 + NBLK)
            for j in range(4):
                sp.dma_start(t["y_sample"][2 * j:2 * j + 2, 0, :], out_rows[32 * j:32 * j + 2, :]).then_inc(out_stored, 16)
            sp.wait_ge(out_stored, 16 * (NBLK - 1 + 4))

        def gather(pool, rows, table, idx, s, landed):
            pool.indirect_dma_start(rows[s][:, :], None, table[0],
                                    bass.IndirectOffsetOnAxis(ap=idx[:, s:s + 1], axis=0)).then_inc(landed[s], 16)

        @block.gpsimd
        def _(pool):
            pool.memset(window[:, :], 0.0).then_inc(const_done, 1)
            pool.memset(pick_row[:, :], 0.0).then_inc(const_done, 1)
            pool.memset(eps[:, :], EPS).then_inc(const_done, 1)
            pool.iota(count_i[:, :], pattern=[[1, TOPK]], base=0, channel_multiplier=0).then_inc(const_done, 1)
            pool.memset(zeros[:, :], 0.0).then_inc(const_done, 1)
            pool.memset(gate2_s[:, :], 0.0).then_inc(const_done, 1)
            pool.wait_ge(const_done, 6)
            pool.memset(window[:, 31:32], 1.0).then_inc(const_done, 1)
            for n in range(3):
                pool.affine_select(out=pick_row[:, :], in_=pick_row[:, :], compare_op=ALU.not_equal, fill=1.0,
                                   base=-32 * n, pattern=[[-1, 32]], channel_multiplier=1).then_inc(const_done, 1)
                pool.wait_ge(const_done, 8 + n)

            def step(n, par, more):
                waits = [(v_idx_ready, n + 1)] + [(u_idx_ready, n + 2)] * more
                for s in range(BODY):
                    wait_apart(pool, pool_noted, (v_used[s], 1 + n), *waits)
                    waits = []
                    gather(pool, v_rows, t["expert_v"], v_idx[par], s, v_landed)
                    if more:
                        wait_apart(pool, pool_noted, (dots_done, 1 + BODY * n + s + 1))
                        gather(pool, u_rows, t["expert_u"], u_idx[1 - par], s, u_landed)

            pool.wait_ge(u_idx_ready, 1)
            for s in range(BODY):
                gather(pool, u_rows, t["expert_u"], u_idx[0], s, u_landed)
            with pool.Fori(0, (NBLK - 1) * HEADS) as m:
                step(2 * m, 0, True)
                step(2 * m + 1, 1, True)
            step((NBLK - 1) * HEADS * 2, 0, False)

        def normalise(act, b):
            act.wait_ge(out_left, 1 + b)
            act.wait_ge(y_done, b + 1)
            nc.scalar.activation(out_rows[:, :], ps_y[:, :], ACT.Square, accum_out=y_stat[:, 0:1]).then_inc(y_ssq, 1)
            act.wait_ge(y_ssq, b + 1)
            nc.scalar.activation(y_stat[:, 1:2], y_stat[:, 0:1], ACT.Sqrt, scale=1.0 / D, bias=eps[:, 0:1]
                                 ).then_inc(y_std, 1)

        @block.scalar
        def _(act):
            act.sem_inc(s_copied, 1)
            act.dma_start(gate2_b[:, :], scratch["mod"][NS:NS + 1, GATE2, :].to_broadcast([P, D])).then_inc(gains_landed, 16)
            act.wait_ge(const_done, 10)
            for j in range(4):
                act.dma_start(gate2_s[32 * j:32 * j + 2, :], scratch["mod"][2 * j:2 * j + 2, GATE2, :]
                              ).then_inc(gains_landed, 16)
            act.dma_start(gain2[:, :], t["g_post_ffn"][0:1, :].to_broadcast([P, D])).then_inc(gains_landed, 16)

            def turn(blk):
                for n, ps in enumerate((ps_a, ps_b)):
                    act.wait_ge(h2_turned, 2 * blk + n + 1)
                    nc.scalar.activation(h2T[:, 4 * n:4 * n + 4, :], ps[:, :, :], ACT.Copy).then_inc(h2T_done, 1)

            def keep_q(hd):
                act.wait_ge(q_done, hd + 1)
                nc.scalar.activation(q_sb[:, :], flat_a[:, 0:QCOLS], ACT.Copy).then_inc(q_copied, 1)

            def keep_qT(hd):
                act.wait_ge(qT_done, hd + 1)
                nc.scalar.activation(qT_sb[:, :], flat_b[:, 0:QCOLS], ACT.Copy).then_inc(qT_copied, 1)

            def keep_s(hd):
                act.wait_ge(s_done, hd + 1)
                act.wait_ge(head_step, CHAIN * hd + SEARCHED)
                nc.scalar.activation(s_sb[:, :, :].rearrange("p a b -> p (a b)"), flat_a[:, 0:QCOLS], ACT.Copy
                                     ).then_inc(s_copied, 1)

            def soften(blk):
                act.wait_ge(soft_step, 4 * blk + 1)
                nc.scalar.activation(gate[:, :, :], gate[:, :, :], ACT.Exp).then_inc(exp_done, 1)

            def finish(blk):
                wait_apart(act, act_noted, (picked_turned, blk + 1))
                dst = expertT[:, ds(blk, 1), :, :].rearrange("p a j i -> p (a j i)")
                nc.scalar.activation(dst, flat_b[:, 0:P], ACT.Copy).then_inc(expert_ready, 1)
                dst = gateT[:, ds(blk, 1), :, :].rearrange("p a j i -> p (a j i)")
                nc.scalar.activation(dst, flat_b[:, P:2 * P], ACT.Copy).then_inc(gate_ready, 1)
                wait_apart(act, act_noted, (expert_ready, blk + 1))

            def index(dst, blk, i0, done):
                src = expertT[:, ds(blk, 1), :, ds(i0, 2)].rearrange("p a j i -> p i (a j)")
                nc.scalar.activation(dst[:, :].rearrange("p (i j) -> p i j", i=2), src, ACT.Copy).then_inc(done, 1)

            def gelu(n, g):
                act.wait_ge(dots_done, 1 + BODY * n + 4 * g + 4)
                act.wait_ge(v_used[4 * g + 3], 1 + n)
                nc.scalar.activation(act_u[g][:, :], dot[g][:, :], ACT.Gelu).then_inc(gelu_done, 1)

            def step(n, par, v_next, u_next, head=None, after_head=None, first=None):
                if first is not None:
                    first()
                if head is not None:
                    keep_q(head)
                gelu(n, 0)
                if head is not None:
                    keep_qT(head)
                    keep_s(head)
                if after_head is not None:
                    after_head()
                if v_next is not None:
                    wait_apart(act, act_noted, (v_used[BODY - 1], 1 + n))
                    index(v_idx[1 - par], *v_next, v_idx_ready)
                gelu(n, 1)
                if u_next is not None:
                    index(u_idx[par], *u_next, u_idx_ready)

            turn(0)
            with act.Fori(0, HEADS) as h:
                keep_q(h)
                keep_qT(h)
                keep_s(h)
            soften(0)
            finish(0)
            index(u_idx[0], 0, 0, u_idx_ready)
            index(u_idx[1], 0, 2, u_idx_ready)
            index(v_idx[0], 0, 0, v_idx_ready)
            step(0, 0, (0, 2), (0, 4))
            with act.Fori(0, NBLK - 1) as b:
                turn(b + 1)
                hd = HEADS * (b + 1)
                with act.Fori(0, PAIRS) as h:
                    step(16 * b + 2 * h + 1, 1, (b, 4 * h + 4), (b, 4 * h + 6), head=hd + h)
                    step(16 * b + 2 * h + 2, 0, (b, 4 * h + 6), (b, 4 * h + 8))
                step(16 * b + 13, 1, (b, 28), (b, 30), head=hd + PAIRS)
                step(16 * b + 14, 0, (b, 30), None, head=hd + PAIRS + 1, after_head=lambda: soften(b + 1))

                def first():
                    finish(b + 1)
                    index(u_idx[0], b + 1, 0, u_idx_ready)

                step(16 * b + 15, 1, (b + 1, 0), (b + 1, 2), first=first)
                step(16 * b + 16, 0, (b + 1, 2), (b + 1, 4))
                normalise(act, b)
            normalise(act, NBLK - 1)

        @block.vector
        def _(dve):
            for primed in (out_done, y_used, dots_done):
                dve.sem_inc(primed, 1)
            dve.sem_inc(head_step, CHAIN)
            dve.wait_ge(gains_landed, 16 * 6)
            dve.tensor_tensor(gate2_b[:, :], gate2_b[:, :], gain2[:, :], ALU.mult).then_inc(gate2_done, 1)
            dve.tensor_tensor(gate2_s[:, :], gate2_s[:, :], gain2[:, :], ALU.mult).then_inc(gate2_done, 1)
            dve.wait_ge(const_done, 10)
            dve.tensor_copy(count[:, :], count_i[:, :]).then_inc(gate2_done, 1)
            dve.wait_ge(gate2_done, 3)

            def retrieve(hd, blk, h):
                own = Steps(dve, head_step, CHAIN * (hd + 1), dve_noted)
                wait_apart(dve, dve_noted, (s_copied, 1 + hd + 1), (picked_turned, blk))
                for p in range(2):
                    own.did(dve.max(top_v[:, p, 0:8], s_sb[:, p, :]))
                for p in range(2):
                    own.settle(back=1)
                    own.did(dve.match_replace(s_less[:, p, :], top_v[:, p, 0:8], s_sb[:, p, :], LOWEST))
                for p in range(2):
                    own.did(dve.max_index(top_i[:, p, 0:8], top_v[:, p, 0:8], s_sb[:, p, :]))
                assert own.n == SEARCHED, own.n
                own.settle(back=2)
                for p in range(2):
                    own.did(dve.max(top_v[:, p, 8:16], s_less[:, p, :]))
                for p in range(2):
                    own.settle(back=1)
                    own.did(dve.max_index(top_i[:, p, 8:16], top_v[:, p, 8:16], s_less[:, p, :]))
                own.did(dve.tensor_tensor(
                    cand[:, :, :], top_v[:, 0, :].rearrange("p (a o) -> p a o", o=1).to_broadcast([P, TOPK, TOPK]),
                    top_v[:, 1:2, :].to_broadcast([P, TOPK, TOPK]), ALU.add))
                own.settle(back=1)
                own.did(dve.tensor_copy(top_f[:, :, :], top_i[:, :, :]))
                flat = cand[:, :, :].rearrange("p a b -> p (a b)")
                hi, lo = pair_v[:, 0:8], pair_v[:, 8:16]
                own.settle(back=1)
                own.did(dve.max(hi, flat))
                own.settle()
                own.did(dve.match_replace(cand_less[:, :], hi, flat, LOWEST))
                own.did(dve.max_index(pair_i[:, 0:8], hi, flat))
                own.settle(back=1)
                own.did(dve.max(lo, cand_less[:, :]))
                own.settle()
                own.did(dve.max_index(pair_i[:, 8:16], lo, cand_less[:, :]))
                own.did(dve.tensor_copy(best[:, ds(h, 1), :].rearrange("p a k -> p (a k)"), pair_v[:, :]))
                own.settle(back=1)
                own.did(dve.tensor_single_scalar(pair_hl[:, 0, :], pair_i[:, :], 4, ALU.logical_shift_right))
                own.did(dve.tensor_single_scalar(pair_hl[:, 1, :], pair_i[:, :], TOPK - 1, ALU.bitwise_and))
                own.settle()
                own.did(dve.tensor_copy(pair_f[:, :, :], pair_hl[:, :, :]))
                own.settle()
                for p in range(2):
                    own.did(dve.tensor_tensor(
                        pick[:, p, :, :], count[:, :].rearrange("p (o r) -> p o r", o=1).to_broadcast([P, TOPK, TOPK]),
                        pair_f[:, p, :].rearrange("p (k o) -> p k o", o=1).to_broadcast([P, TOPK, TOPK]),
                        ALU.is_equal))
                for p in range(2):
                    own.settle(back=1)
                    own.did(dve.tensor_tensor(
                        pick[:, p, :, :], pick[:, p, :, :],
                        top_f[:, p:p + 1, :].to_broadcast([P, TOPK, TOPK]), ALU.mult))
                for p in range(2):
                    own.settle(back=1)
                    own.did(dve.tensor_reduce(pick_f[:, p, :], pick[:, p, :, :], AX, ALU.add))
                own.settle()
                own.did(dve.scalar_tensor_tensor(out=expert_f[:, ds(h * TOPK, TOPK)], in0=pick_f[:, 0, :],
                                                 scalar=float(KEYS), in1=pick_f[:, 1, :], op0=ALU.mult, op1=ALU.add))
                own.settle()
                assert own.n == CHAIN, own.n

            def center(blk):
                own = Steps(dve, soft_step, 4 * blk)
                own.did(dve.tensor_tensor(gate[:, :, :], best[:, :, :], best[:, :, 0:1].to_broadcast([P, HEADS, TOPK]),
                                          ALU.subtract))

            def soften(blk):
                own = Steps(dve, soft_step, 4 * blk + 1)
                dve.wait_ge(exp_done, blk + 1)
                own.did(dve.tensor_reduce(total[:, :], gate[:, :, :], AX, ALU.add))
                own.settle()
                own.did(dve.reciprocal(inverse[:, :], total[:, :]))
                own.settle()
                own.did(dve.tensor_tensor(gate[:, :, :], gate[:, :, :],
                                          inverse[:, :].rearrange("p (h o) -> p h o", o=1).to_broadcast([P, HEADS, TOPK]),
                                          ALU.mult))

            def product(n, s):
                dve.wait_ge(x_spread, BODY * n + s + 1)
                dve.wait_ge(u_landed[s], 16 * n + 16)
                dve.tensor_tensor_reduce(u_rows[s][:, :], u_rows[s][:, :], ps_x[s % 2][:, :], 1.0, 0.0, ALU.mult,
                                         ALU.add, dot[s // 4][:, s % 4:s % 4 + 1]).then_inc(dots_done, 1)

            def weigh(n, blk, i0, g):
                dve.wait_ge(gelu_done, 2 * n + g + 1)
                i = i0 + g
                for j in range(4):
                    s = 4 * g + j
                    dve.wait_ge(v_used[s], 1 + n)
                    scale = gateT[:, ds(blk, 1), j, ds(i, 1)].rearrange("p a i -> p (a i)")
                    dve.tensor_scalar(weight[s][:, :], window[:, ds(31 - i, 32)], act_u[g][:, j:j + 1], scale,
                                      ALU.mult, ALU.mult).then_inc(weight_done, 1)

            def step(n, here, before, head=None, last=False):
                product(n, 0)
                if before is not None:
                    weigh(n - 1, *before, 1)
                for s in (1, 2, 3, 4, 5):
                    product(n, s)
                    if s == 4:
                        weigh(n, *here, 0)
                if head is not None:
                    retrieve(*head)
                if last:
                    center(head[1])
                product(n, 6)
                if last:
                    soften(head[1])
                product(n, 7)

            def emit(b, gate2):
                dve.wait_ge(y_std, b + 1)
                dve.reciprocal(y_stat[:, 2:3], y_stat[:, 1:2]).then_inc(y_inverse, 1)
                dve.wait_ge(y_inverse, b + 1)
                dve.scalar_tensor_tensor(out=out_rows[:, :], in0=ps_y[:, :], scalar=y_stat[:, 2:3], in1=gate2[:, :],
                                         op0=ALU.mult, op1=ALU.mult).then_inc(y_used, 1)
                dve.wait_ge(y_used, 1 + b + 1)
                dve.wait_ge(x1_landed, 16 * b + 16)
                if gate2 is gate2_s:
                    dve.wait_ge(x1_landed, 16 * b + 64)
                dve.tensor_tensor(out_rows[:, :], out_rows[:, :], x1_in[:, :], ALU.add).then_inc(out_done, 1)

            with dve.Fori(0, HEADS // 2) as pair:
                retrieve(2 * pair, 0, 2 * pair)
                retrieve(2 * pair + 1, 0, 2 * pair + 1)
            center(0)
            soften(0)
            dve.wait_ge(gate_ready, 1)
            step(0, (0, 0), None)
            with dve.Fori(0, NBLK - 1) as b:
                hd = HEADS * (b + 1)
                with dve.Fori(0, PAIRS) as h:
                    step(16 * b + 2 * h + 1, (b, 4 * h + 2), (b, 4 * h), head=(hd + h, b + 1, h))
                    step(16 * b + 2 * h + 2, (b, 4 * h + 4), (b, 4 * h + 2))
                step(16 * b + 13, (b, 26), (b, 24), head=(hd + PAIRS, b + 1, PAIRS))
                step(16 * b + 14, (b, 28), (b, 26), head=(hd + PAIRS + 1, b + 1, PAIRS + 1), last=True)
                step(16 * b + 15, (b, 30), (b, 28))
                step(16 * b + 16, (b + 1, 0), (b, 30))
                emit(b, gate2_b)
            weigh(16 * (NBLK - 1), NBLK - 1, 0, 1)
            emit(NBLK - 1, gate2_s)

        @block.tensor
        def _(pe):
            for primed in v_used:
                pe.sem_inc(primed, 1)
            def turn(blk):
                pe.wait_ge(h2_landed, 16 * blk + 16)
                for n, ps in enumerate((ps_a, ps_b)):
                    if n == 0:
                        pe.wait_ge(s_copied, 1 + HEADS * blk)
                    else:
                        pe.wait_ge(gate_ready, blk)
                    for k in range(4):
                        last = pe.transpose(ps[:, k, :], h2_in[:, (4 * n + k) * P:(4 * n + k + 1) * P], ident[:, :])
                    last.then_inc(h2_turned, 1)

            def queries(hd, blk, h):
                pe.wait_ge(h2T_done, 2 * blk + 2)
                pe.wait_ge(s_copied, 1 + hd)
                for k in range(KD):
                    last = pe.matmul(flat_a[:, 0:QCOLS], h2T[:, k, :], w_q[:, k, ds(h * QCOLS, QCOLS)],
                                     start=(k == 0), stop=(k == KD - 1))
                last.then_inc(q_done, 1)

            def turn_queries(hd):
                pe.wait_ge(q_copied, hd + 1)
                for p in range(2):
                    last = pe.transpose(flat_b[:, p * P:(p + 1) * P], q_sb[:, p * P:(p + 1) * P], ident[:, :])
                last.then_inc(qT_done, 1)

            def scores(hd, h):
                pe.wait_ge(qT_copied, hd + 1)
                for p in range(2):
                    last = pe.matmul(flat_a[:, p * P:(p + 1) * P], qT_sb[:, p * P:(p + 1) * P],
                                     keysT[:, ds(2 * h + p, 1), :].rearrange("p a k -> p (a k)"), start=True, stop=True)
                last.then_inc(s_done, 1)

            def finish(blk):
                pe.wait_ge(head_step, CHAIN * (HEADS * (blk + 1) + 1))
                pe.wait_ge(soft_step, 4 * blk + 4)
                pe.transpose(flat_b[:, 0:P], expert_f[:, :], ident[:, :])
                pe.transpose(flat_b[:, P:2 * P], gate[:, :, :].rearrange("p h k -> p (h k)"), ident[:, :]
                             ).then_inc(picked_turned, 1)

            def spread(n, s, blk, i):
                for c in range(2):
                    src = h2_bf[:, ds(blk % 2, 1), s % 4, c * HALF:(c + 1) * HALF].rearrange("p a d -> p (a d)")
                    last = pe.matmul(ps_x[s % 2][:, c * HALF:(c + 1) * HALF], pick_row[:, ds(i, 1)].to_broadcast([96, P]),
                                     src, start=True, stop=True)
                last.then_inc(x_spread, 1)

            def gather_sum(n, s):
                pe.wait_ge(weight_done, BODY * n + s + 1)
                pe.wait_ge(v_landed[s], 16 * n + 16)
                j = 32 * (s % 4)
                for c in range(2):
                    last = pe.matmul(ps_y[j:j + 32, c * HALF:(c + 1) * HALF], weight[s][:, :],
                                     v_rows[s][:, c * HALF:(c + 1) * HALF], start=False, stop=False,
                                     skip_group_check=True)
                last.then_inc(v_used[s], 1)

            def step(n, here, after, head=None, sums=True, picked=None):
                for s in range(BODY):
                    if sums:
                        gather_sum(n - 1, s)
                    pe.wait_ge(dots_done, 1 + BODY * n + s + 1)
                    if s + 2 < BODY:
                        spread(n, s + 2, here[0], here[1] + (s + 2) // 4)
                    elif after is not None:
                        spread(n + 1, s + 2 - BODY, *after)
                    if picked is not None and s == 0:
                        finish(picked)
                    if head is not None:
                        if s == 0:
                            queries(*head)
                        if s == 3:
                            turn_queries(head[0])
                        if s == 4:
                            scores(head[0], head[2])

            def bound(first):
                for c in range(2):
                    last = pe.matmul(ps_y[:, c * HALF:(c + 1) * HALF], zeros[:, 0:P], zeros[:, :], start=first,
                                     stop=not first, skip_group_check=True)
                return last

            turn(0)
            with pe.Fori(0, HEADS) as h:
                queries(h, 0, h)
                turn_queries(h)
                scores(h, h)
            finish(0)
            pe.wait_ge(bf_landed, 48)
            pe.wait_ge(const_done, 10)
            spread(0, 0, 0, 0)
            spread(0, 1, 0, 0)
            step(0, (0, 0), (0, 2), sums=False)
            with pe.Fori(0, NBLK - 1) as b:
                turn(b + 1)
                pe.wait_ge(y_used, 1 + b)
                bound(True)
                hd = HEADS * (b + 1)
                with pe.Fori(0, PAIRS) as h:
                    step(16 * b + 2 * h + 1, (b, 4 * h + 2), (b, 4 * h + 4), head=(hd + h, b + 1, h))
                    step(16 * b + 2 * h + 2, (b, 4 * h + 4), (b, 4 * h + 6))
                step(16 * b + 13, (b, 26), (b, 28), head=(hd + PAIRS, b + 1, PAIRS))
                step(16 * b + 14, (b, 28), (b, 30), head=(hd + PAIRS + 1, b + 1, PAIRS + 1))
                pe.wait_ge(bf_landed, 48 * b + 96)
                step(16 * b + 15, (b, 30), (b + 1, 0), picked=b + 1)
                step(16 * b + 16, (b + 1, 0), (b + 1, 2))
                bound(False).then_inc(y_done, 1)
            pe.wait_ge(y_used, 1 + NBLK - 1)
            bound(True)
            for s in range(BODY):
                gather_sum(16 * (NBLK - 1), s)
            bound(False).then_inc(y_done, 1)


_INS = ["x_prompt", "x_sample", "state_conv", "c_prompt", "c_sample", "w_ada", "b_ada", "g_pre_mix", "w_in", "conv_w",
        "sgu_norm_g", "w_s", "b_s", "w_out", "g_post_mix", "g_pre_ffn", "w_q", "sub_keys", "expert_u", "expert_v",
        "g_post_ffn"]
_OUTS = [("y_prompt", (1, SEQ, D)), ("y_sample", (NS, 1, D)), ("new_conv_prompt", (1, 1, 2, CONV)),
         ("new_conv_sample", (1, NS, 2, CONV)), ("sgu_v_sample", (1, NS, 1, CONV))]


def kernel(**inputs):
    import concourse.bacc as _bacc
    from concourse.bass_utils import run_bass_kernel_spmd as _run

    nc = _bacc.Bacc("TRN2", target_bir_lowering=False, num_devices=1)
    arrays, t = {}, {}
    for name in _INS:
        a = np.ascontiguousarray(inputs[name])
        arrays[f"in_{name}_dram"] = a
        t[name] = nc.dram_tensor(f"in_{name}_dram", a.shape, mybir.dt.from_np(a.dtype), kind="ExternalInput").ap()
    for name, shape in _OUTS:
        t[name] = nc.dram_tensor(f"out_{name}_dram", shape, F32, kind="ExternalOutput").ap()
    build(nc, t)
    r = _run(nc, [arrays], core_ids=[0])
    return tuple(r.results[0][f"out_{name}_dram"] for name, _ in _OUTS)
```
